# Optimizing a Trainium2 kernel written in Bass

```python
import math
import jax, jax.numpy as jnp
from jax import lax
import numpy as np

D_MODEL = 1024
BATCH = 1
SEQ = 512
DEPTH = 2
DEC_BATCH = 1
DEC_SEQ = 512
PAST_LEN = 128

N_MIXERS = 2
N_POOL_LAYERS = (DEPTH + 1) // 2
N_ATTN_LAYERS = DEPTH // 2
POOL_WINDOWS = (2, 4, 8, 16)
N_POOL_GROUPS = len(POOL_WINDOWS)
POOL_GROUP_DIM = D_MODEL // N_POOL_GROUPS
HEAD_DIM = 128
N_HEADS = D_MODEL // HEAD_DIM
N_KV_HEADS = 2
GQA_GROUP = N_HEADS // N_KV_HEADS
QKV_DIM = (N_HEADS + 2 * N_KV_HEADS) * HEAD_DIM
ROPE_AXIS_DIM = HEAD_DIM // 2
ROPE_THETA = 10000.0
GRID_W = 64
Q_BLOCK = 128
D_FF = int(math.ceil(8 * D_MODEL / 3 / 256) * 256)
EPS = 1e-6

kernel_name = "hybrid_pool_gqa_axialrope_encoder"

def rms_norm(x, g):
    xf = x.astype(jnp.float32)
    y = xf * lax.rsqrt(jnp.mean(xf * xf, axis=-1, keepdims=True) + EPS)
    return (y * g.astype(jnp.float32)).astype(x.dtype)

def pool_mixer(h, w_pool, b_pool, scale):
    B, T, D = h.shape
    hf = h.astype(jnp.float32)
    cs = jnp.concatenate([jnp.zeros((B, 1, D), jnp.float32), jnp.cumsum(hf, axis=1)], axis=1)
    t = jnp.arange(T, dtype=jnp.int32)
    outs = []
    for gi, w in enumerate(POOL_WINDOWS):
        sl = slice(gi * POOL_GROUP_DIM, (gi + 1) * POOL_GROUP_DIM)
        lo = jnp.maximum(t - w // 2, 0)
        hi = jnp.minimum(t + w // 2, T)
        csg = cs[:, :, sl]
        window_sum = jnp.take(csg, hi, axis=1) - jnp.take(csg, lo, axis=1)
        count = (hi - lo).astype(jnp.float32)[None, :, None]
        pooled = window_sum / count - hf[:, :, sl]
        y = jnp.einsum('btc,cd->btd', pooled, w_pool[gi].astype(jnp.float32)) + b_pool[gi].astype(jnp.float32)
        outs.append(y)
    y = jnp.concatenate(outs, axis=-1) * scale.astype(jnp.float32)
    return y.astype(h.dtype)

def axial_rope_tables(T):
    rows = T // GRID_W
    rr, cc = jnp.meshgrid(jnp.arange(rows, dtype=jnp.float32), jnp.arange(GRID_W, dtype=jnp.float32), indexing='ij')
    row = rr.reshape(-1)
    col = cc.reshape(-1)
    inv_freq = ROPE_THETA ** (-jnp.arange(0, ROPE_AXIS_DIM, 2, dtype=jnp.float32) / ROPE_AXIS_DIM)
    ang_r = row[:, None] * inv_freq[None, :]
    ang_c = col[:, None] * inv_freq[None, :]
    ang_r = jnp.concatenate([ang_r, ang_r], axis=-1)
    ang_c = jnp.concatenate([ang_c, ang_c], axis=-1)
    return jnp.cos(ang_r), jnp.sin(ang_r), jnp.cos(ang_c), jnp.sin(ang_c)

def rotate_half(x):
    x1, x2 = jnp.split(x, 2, axis=-1)
    return jnp.concatenate([-x2, x1], axis=-1)

def apply_axial_rope(x, tables):
    cos_r, sin_r, cos_c, sin_c = tables
    xf = x.astype(jnp.float32)
    xr, xc = xf[..., :ROPE_AXIS_DIM], xf[..., ROPE_AXIS_DIM:]
    cr, sr = cos_r[None, :, None, :], sin_r[None, :, None, :]
    cc, sc = cos_c[None, :, None, :], sin_c[None, :, None, :]
    yr = xr * cr + rotate_half(xr) * sr
    yc = xc * cc + rotate_half(xc) * sc
    return jnp.concatenate([yr, yc], axis=-1).astype(x.dtype)

def attention_mixer(h, w_qkv, q_gain, k_gain, w_o):
    B, T, D = h.shape
    qkv = jnp.einsum('btd,de->bte', h, w_qkv)
    q = qkv[..., :N_HEADS * HEAD_DIM].reshape(B, T, N_HEADS, HEAD_DIM)
    k = qkv[..., N_HEADS * HEAD_DIM:(N_HEADS + N_KV_HEADS) * HEAD_DIM].reshape(B, T, N_KV_HEADS, HEAD_DIM)
    v = qkv[..., (N_HEADS + N_KV_HEADS) * HEAD_DIM:].reshape(B, T, N_KV_HEADS, HEAD_DIM)
    q = rms_norm(q, q_gain)
    k = rms_norm(k, k_gain)
    tables = axial_rope_tables(T)
    q = apply_axial_rope(q, tables)
    k = apply_axial_rope(k, tables)
    n_blk = T // Q_BLOCK
    qb = q.reshape(B, n_blk, Q_BLOCK, N_KV_HEADS, GQA_GROUP, HEAD_DIM).transpose(1, 0, 2, 3, 4, 5)
    scale = 1.0 / math.sqrt(HEAD_DIM)

    def one_block(q_blk):
        s = jnp.einsum('bqkgd,bskd->bkgqs', q_blk, k).astype(jnp.float32) * scale
        p = jax.nn.softmax(s, axis=-1)
        return jnp.einsum('bkgqs,bskd->bqkgd', p.astype(v.dtype), v)

    o = lax.map(one_block, qb)
    o = o.transpose(1, 0, 2, 3, 4, 5).reshape(B, T, N_HEADS * HEAD_DIM)
    return jnp.einsum('bte,ed->btd', o, w_o)

def swiglu_ffn(h, w_gate_up, w_down):
    gu = jnp.einsum('btd,df->btf', h, w_gate_up)
    g, u = gu[..., :D_FF], gu[..., D_FF:]
    return jnp.einsum('btf,fd->btd', jax.nn.silu(g) * u, w_down)

def trunk(x, norm_mix, norm_ffn, pool_w, pool_b, pool_scale,
          attn_w_qkv, attn_q_gain, attn_k_gain, attn_w_o, ffn_w_gate_up, ffn_w_down):
    for i in range(DEPTH):
        h = rms_norm(x, norm_mix[i])
        j = i // N_MIXERS
        if i % N_MIXERS == 0:
            x = x + pool_mixer(h, pool_w[j], pool_b[j], pool_scale[j])
        else:
            x = x + attention_mixer(h, attn_w_qkv[j], attn_q_gain[j], attn_k_gain[j], attn_w_o[j])
        h = rms_norm(x, norm_ffn[i])
        x = x + swiglu_ffn(h, ffn_w_gate_up[i], ffn_w_down[i])
    return x

def setup_inputs(seed: int = 0) -> dict:
    key = jax.random.key(seed)
    ks = jax.random.split(key, 16)
    f32 = jnp.float32
    nrm = lambda k, shape, s: jax.random.normal(k, shape, f32) * s
    return {
        "x_prompt": nrm(ks[0], (BATCH, SEQ, D_MODEL), 1.0),
        "x_sample": nrm(ks[1], (DEC_BATCH, DEC_SEQ, D_MODEL), 1.0),
        "norm_mix": 1.0 + nrm(ks[2], (DEPTH, D_MODEL), 0.05),
        "norm_ffn": 1.0 + nrm(ks[3], (DEPTH, D_MODEL), 0.05),
        "pool_w": nrm(ks[4], (N_POOL_LAYERS, N_POOL_GROUPS, POOL_GROUP_DIM, POOL_GROUP_DIM), POOL_GROUP_DIM ** -0.5),
        "pool_b": nrm(ks[5], (N_POOL_LAYERS, N_POOL_GROUPS, POOL_GROUP_DIM), 0.02),
        "pool_scale": 1.0 + nrm(ks[6], (N_POOL_LAYERS, D_MODEL), 0.1),
        "attn_w_qkv": nrm(ks[7], (N_ATTN_LAYERS, D_MODEL, QKV_DIM), D_MODEL ** -0.5),
        "attn_q_gain": 1.0 + nrm(ks[8], (N_ATTN_LAYERS, HEAD_DIM), 0.05),
        "attn_k_gain": 1.0 + nrm(ks[9], (N_ATTN_LAYERS, HEAD_DIM), 0.05),
        "attn_w_o": nrm(ks[10], (N_ATTN_LAYERS, N_HEADS * HEAD_DIM, D_MODEL), (N_HEADS * HEAD_DIM) ** -0.5),
        "ffn_w_gate_up": nrm(ks[11], (DEPTH, D_MODEL, 2 * D_FF), D_MODEL ** -0.5),
        "ffn_w_down": nrm(ks[12], (DEPTH, D_FF, D_MODEL), D_FF ** -0.5),
    }

def reference(x_prompt, x_sample, norm_mix, norm_ffn, pool_w, pool_b, pool_scale,
              attn_w_qkv, attn_q_gain, attn_k_gain, attn_w_o, ffn_w_gate_up, ffn_w_down):
    y_prompt = trunk(x_prompt, norm_mix, norm_ffn, pool_w, pool_b, pool_scale,
                     attn_w_qkv, attn_q_gain, attn_k_gain, attn_w_o, ffn_w_gate_up, ffn_w_down)
    y_sample = trunk(x_sample, norm_mix, norm_ffn, pool_w, pool_b, pool_scale,
                     attn_w_qkv, attn_q_gain, attn_k_gain, attn_w_o, ffn_w_gate_up, ffn_w_down)
    return (y_prompt, y_sample)


_drawn_inputs = setup_inputs


def setup_inputs(seed=0):
    import zlib

    import numpy as np

    out = dict(_drawn_inputs(seed))
    spreads = {}
    factors = {'attn_q_gain': 8.0, 'attn_k_gain': 8.0}
    for name, (base, spread) in spreads.items():
        noise = np.random.default_rng([zlib.crc32(name.encode()), seed]).standard_normal(out[name].shape)
        drawn = base * np.exp(spread * noise) if base else spread * noise
        out[name] = __import__('jax').numpy.asarray(drawn.astype(out[name].dtype))
    for name, factor in factors.items():
        out[name] = (out[name] * factor).astype(out[name].dtype)
    return out
```

```python
from contextlib import ExitStack

import concourse.bass as bass
from concourse import mybir

F32 = mybir.dt.float32
F32R = mybir.dt.float32r
ALU = mybir.AluOpType
ACT = mybir.ActivationFunctionType
AX = mybir.AxisListType

P = 128
D = 1024
KC = D // P
T = 512
NB = 2
DFF = 2816
NF = DFF // P
GF = 2
NG = NF // GF
HEADS, KVH, HD = 8, 2, 128
EPS = 1e-6
WINDOWS = (2, 4, 8, 16)
PAD = 8
TP = T + 2 * PAD
EDGE = 8

UNIT = 1024
RAW = 3
RING = 6
U_POOL = 0
U_FFN0 = U_POOL + 2
N_FFN = NG * 3 * GF
U_QKV = U_FFN0 + N_FFN
U_WO = U_QKV + 2 * KVH + HEADS
U_FFN1 = U_WO + KC
U_END = U_FFN1 + N_FFN
U_FFN = (U_FFN0, U_FFN1)
N_TILE = NG * GF * NB
N_DOWN = NG * KC * NB
BODIES = 2
LOOPS = (NG - 2) // BODIES
FIRST_PEELED = 1 + LOOPS * BODIES

V_MIX, V_FFN, V_PB, V_PS, V_QG, V_KG = 0, 16, 32, 40, 48, 49
N_VEC = 50
V_BS = 50


def build(nc, x_prompt, x_sample, norm_mix, norm_ffn, pool_w, pool_b, pool_scale, w_qkv, q_gain,
          k_gain, w_o, w_gu, w_down, rope_cos, rope_sin, edge_tab, y_prompt, y_sample):
    with ExitStack() as ctx:
        base = (nc.sbuf_base + 31) // 32 * 32
        top = [base]

        def at(name, shape, dt, off):
            return nc.alloc_sbuf_tensor_at(name, shape, dt, offset=off)

        def take(nbytes):
            off = top[0]
            top[0] += nbytes
            return off

        o_x, o_h, o_act = take(KC * NB * T * 4), take(KC * NB * T * 8), take(32768)
        o_ring, o_raw, o_tmp = take(RING * UNIT * 8), take(RAW * UNIT * 4), take(8 * T * 4)
        o_const = take(0)
        x = at("x", [P, KC, NB * T], F32, o_x)
        h_hi = at("h_hi", [P, KC, NB * T], F32R, o_h)
        h_lo = at("h_lo", [P, KC, NB * T], F32R, o_h + 32768)
        act_hi = at("act_hi", [P, 2, GF, NB * T], F32R, o_act)
        act_lo = at("act_lo", [P, 2, GF, NB * T], F32R, o_act + 16384)
        k_hi = at("k_hi", [P, KVH, NB * T], F32R, o_act)
        k_lo = at("k_lo", [P, KVH, NB * T], F32R, o_act + 8192)
        v_hi = at("v_hi", [P, NB * T // P, KVH * HD], F32R, o_act + 16384)
        v_lo = at("v_lo", [P, NB * T // P, KVH * HD], F32R, o_act + 24576)
        hp = [at(f"hp{i}", [P, TP], F32, o_act + i * TP * 4) for i in range(4)]
        wsum = [at(f"wsum{i}", [P, TP], F32, o_act + (4 + i) * TP * 4) for i in range(2)]
        wsum_pool = [at(f"wsum_pool{i}", [P, TP], F32, o_act + (6 + i) * TP * 4) for i in range(4)]
        w_hi_t = at("w_hi_t", [P, RING, UNIT], F32R, o_ring)
        w_lo_t = at("w_lo_t", [P, RING, UNIT], F32R, o_ring + RING * UNIT * 4)
        raw = at("raw", [P, RAW, UNIT], F32, o_raw)
        xin = at("xin", [P, NB * T // P, D], F32, o_h)
        yout = at("yout", [P, NB * T // P, D], F32, o_h)
        tmp = [at(f"tmp{i}", [P, T], F32, o_tmp + i * T * 4) for i in range(8)]
        silu_t, full, sqr, stat = tmp[0:2], tmp[2:4], tmp[4:6], tmp[6:8]
        qg, rot, qsq, cos_t, sin_t = tmp[0:2], tmp[2:4], tmp[4:6], tmp[6], tmp[7]
        vec_in = at("vec_in", [N_VEC, P], F32, o_tmp)
        q_store = [at(f"q_store{i}", [P, HEADS // 2, NB * T], F32, o_ring + i * RING * UNIT * 4 + 2 * UNIT * 4)
                   for i in range(2)]
        prob = at("prob", [P, 4, T], F32, o_h)
        pt_hi = at("pt_hi", [P, 4, T], F32R, o_h + 8192)
        pt_lo = at("pt_lo", [P, 4, T], F32R, o_h + 16384)
        qs_hi = at("qs_hi", [P, 2, T], F32R, o_h + 24576)
        qs_lo = at("qs_lo", [P, 2, T], F32R, o_h + 28672)
        o_hi = [at("o_hi0", [P, HEADS, T], F32R, o_h + 32768), at("o_hi1", [P, HEADS, T], F32R, o_h)]
        o_lo = [at("o_lo0", [P, HEADS, T], F32R, o_h + 49152), at("o_lo1", [P, HEADS, T], F32R, o_h + 16384)]
        ident = at("ident", [P, P], F32, o_const)
        ones = at("ones", [P, P], F32, o_const + 512)
        vec = at("vec", [P, 64], F32, o_const + 1024)
        edge = at("edge", [P, len(WINDOWS), 2, EDGE], F32, o_const + 1280)
        nmax = at("nmax", [P, 8], F32, o_const + 1536)
        rsum = at("rsum", [P, 8], F32, o_const + 1568)
        rinv = at("rinv", [P, 8], F32, o_const + 1600)
        epst = at("epst", [P, 2], F32, o_const + 1632)
        assert o_const + 1664 <= nc.sbuf_usable_end, (o_const, nc.sbuf_usable_end)

        bank = [ctx.enter_context(nc.psum_tensor(f"bank{i}", [P, T], F32)) for i in range(8)]
        b_gate, b_up, b_down = bank[0:2], bank[2:4], bank[4:8]

        def sem(name):
            return ctx.enter_context(nc.semaphore(name))

        x_in = [sem(f"x_in{i}") for i in range(NB * T // P)]
        vec_landed, edge_landed = sem("vec_landed"), sem("edge_landed")
        ident_made, ones_made, pads_made, eps_made = sem("ident_made"), sem("ones_made"), sem("pads_made"), sem("eps_made")
        vec_turned, vec_ready = sem("vec_turned"), sem("vec_ready")
        x_turned, x_copied_act, x_copied_dve = sem("x_turned"), sem("x_copied_act"), sem("x_copied_dve")
        raw_in = [sem(f"raw_in{i}") for i in range(RAW)]
        w_hi, w_lo = sem("w_hi"), sem("w_lo")
        n_sq, n_acc, n_ms, n_sqrt = sem("n_sq"), sem("n_acc"), sem("n_ms"), sem("n_sqrt")
        n_rstd, n_full, n_hi, n_lo = sem("n_rstd"), sem("n_full"), sem("n_hi"), sem("n_lo")
        m_row, m_step, m_pstep, m_psum = sem("m_row"), sem("m_step"), sem("m_pstep"), sem("m_psum")
        m_full, m_hi, m_lo = sem("m_full"), sem("m_hi"), sem("m_lo")
        m_filled, m_scaled, m_x = sem("m_filled"), sem("m_scaled"), sem("m_x")
        gate_done, up_done, silu_done, prod_done = sem("gate_done"), sem("up_done"), sem("silu_done"), sem("prod_done")
        act_hi_done, act_lo_done = sem("act_hi_done"), sem("act_lo_done")
        down_filled, down_added = sem("down_filled"), sem("down_added")
        proj_done, p_sq, p_gain, p_ms, p_sqrt = sem("proj_done"), sem("p_sq"), sem("p_gain"), sem("p_ms"), sem("p_sqrt")
        rot_in = [sem("rot_in0"), sem("rot_in1")]
        p_r, p_cos, p_sin, p_sum, p_fin, p_hi, p_done = (sem("p_r"), sem("p_cos"), sem("p_sin"), sem("p_sum"),
                                                        sem("p_fin"), sem("p_hi"), sem("p_done"))
        v_filled, v_hi_done, v_lo_done, tables_in = sem("v_filled"), sem("v_hi_done"), sem("v_lo_done"), sem("tables_in")
        a_qhi, a_q, s_filled, a_max, a_exp = sem("a_qhi"), sem("a_q"), sem("s_filled"), sem("a_max"), sem("a_exp")
        a_rinv, a_prob, pt_filled, a_pthi, a_ptlo = sem("a_rinv"), sem("a_prob"), sem("pt_filled"), sem("a_pthi"), sem("a_ptlo")
        o_filled, o_copied = sem("o_filled"), sem("o_copied")
        o0_hi, o0_split, o1_hi, o1_split = sem("o0_hi"), sem("o0_split"), sem("o1_hi"), sem("o1_split")
        wo_filled, wo_added = sem("wo_filled"), sem("wo_added")
        y_turned, y_act, y_dve, y_out = sem("y_turned"), sem("y_act"), sem("y_dve"), sem("y_out")

        block = ctx.enter_context(nc.Block())

        def tok(b):
            return slice(b * T, (b + 1) * T)

        def slot(u):
            if U_QKV <= u < U_FFN1:
                return (u - U_QKV) % 2
            if u >= U_FFN1:
                return (u - U_FFN1) % RING
            return (u - U_FFN0) % RING

        def gu_unit(layer, g, c, up):
            return U_FFN[layer] + (0 if g == 0 else 4 + 6 * (g - 1)) + 2 * c + up

        def down_unit(layer, g, c):
            return U_FFN[layer] + (4 + 6 * g + 4 if g < NG - 1 else N_FFN - 2) + c

        def q_of(h, b):
            return q_store[h // 4][:, h % 4, tok(b)]

        gu_rows = [w_gu[l].rearrange("(k p) f -> p k f", p=P) for l in range(2)]
        qkv_rows = w_qkv[0].rearrange("(k p) e -> p k e", p=P)
        wo_rows = w_o[0].rearrange("(k p) e -> p k e", p=P)

        @block.sync
        def _(sp):
            def load_unit(u, src, shape, w_lo_before=None):
                if w_lo_before is not None:
                    sp.wait_ge(w_lo, w_lo_before)
                elif u >= RAW:
                    sp.wait_ge(w_lo, u - RAW + 1)
                dst = raw[:, u % RAW, :]
                if shape:
                    dst = dst.rearrange("p (k f) -> p k f", k=shape)
                sp.dma_start(dst, src).then_inc(raw_in[u % RAW], 16)

            def load_gu(layer, g, j=None, g0=None):
                for c in range(GF):
                    for up in range(2):
                        u = gu_unit(layer, g if j is None else g0, c, up)
                        if j is None:
                            col = up * DFF + (GF * g + c) * P
                            load_unit(u, gu_rows[layer][:, :, col:col + P], KC)
                        else:
                            col = j * (BODIES * GF * P) + up * DFF + (GF * g0 + c) * P
                            load_unit(u, gu_rows[layer][:, :, bass.ds(col, P)], KC,
                                      j * (6 * BODIES) + u - RAW + 1)

            def load_down(layer, g, j=None, g0=None):
                for c in range(GF):
                    u = down_unit(layer, g if j is None else g0, c)
                    if j is None:
                        r = (GF * g + c) * P
                        load_unit(u, w_down[layer][r:r + P, :], 0)
                    else:
                        r = j * (BODIES * GF * P) + (GF * g0 + c) * P
                        load_unit(u, w_down[layer][bass.ds(r, P), :], 0, j * (6 * BODIES) + u - RAW + 1)

            def load_ffn(layer, skip=0):
                load_gu(layer, 0)
                with sp.Fori(0, LOOPS) as j:
                    for g0 in range(1, 1 + BODIES):
                        load_gu(layer, None, j, g0)
                        load_down(layer, None, j, g0 - 1)
                for g in range(FIRST_PEELED, NG):
                    load_gu(layer, g)
                    load_down(layer, g - 1)
                load_down(layer, NG - 1)

            for row, src in ((V_MIX, norm_mix.rearrange("l (c p) -> (l c) p", p=P)),
                             (V_FFN, norm_ffn.rearrange("l (c p) -> (l c) p", p=P)),
                             (V_PB, pool_b.rearrange("l g (c p) -> (l g c) p", p=P)),
                             (V_PS, pool_scale.rearrange("l (c p) -> (l c) p", p=P)),
                             (V_QG, q_gain), (V_KG, k_gain)):
                sp.dma_start(vec_in[row:row + src.shape[0], :], src).then_inc(vec_landed, 16)
            for i in range(NB * T // P):
                src = (x_prompt, x_sample)[i // 4][0]
                r = (i % 4) * P
                sp.dma_start(xin[:, i, :], src[r:r + P, :]).then_inc(x_in[i], 16)
            sp.dma_start(edge[:, :, :, :], edge_tab).then_inc(edge_landed, 16)
            for i in range(2):
                sp.dma_start(raw[:, i, :].rearrange("p (g k e) -> p g k e", g=2, k=2),
                             pool_w[0, 2 * i:2 * i + 2].rearrange("g (k p) e -> p g k e", p=P)
                             ).then_inc(raw_in[i], 16)
            load_ffn(0)

            def load_qkv(i):
                u = U_QKV + i
                if i < 2:
                    load_unit(u, qkv_rows[:, :, (HEADS + i) * HD:(HEADS + i + 1) * HD], KC)
                elif i < 4:
                    k0 = (i - 2) * 4
                    load_unit(u, qkv_rows[:, k0:k0 + 4, (HEADS + KVH) * HD:], 4)
                else:
                    load_unit(u, qkv_rows[:, :, (i - 4) * HD:(i - 3) * HD], KC)

            def load_wo(m):
                load_unit(U_WO + m, wo_rows[:, :, m * P:(m + 1) * P], KC)

            def rotate(idx):
                sp.wait_ge(p_gain, idx + 1)
                for dst, src in ((0, 1), (1, 0), (2, 3), (3, 2)):
                    sp.dma_start(rot[idx % 2][32 * dst:32 * dst + 32, :],
                                 qg[idx % 2][32 * src:32 * src + 32, :]).then_inc(rot_in[idx % 2], 16)

            for i in range(RAW):
                load_qkv(i)
            sp.wait_ge(n_full, 2 * 16)
            sp.dma_start(cos_t[:, :], rope_cos).then_inc(tables_in, 16)
            sp.dma_start(sin_t[:, :], rope_sin).then_inc(tables_in, 16)
            sp.wait_ge(n_lo, 2 * 16)
            rotate(0)
            rotate(1)
            load_qkv(3)
            rotate(2)
            rotate(3)
            load_qkv(4)
            load_qkv(5)
            load_qkv(6)
            for h in range(HEADS):
                rotate(4 + 2 * h)
                rotate(5 + 2 * h)
                if 7 + h < 12:
                    load_qkv(7 + h)
                elif 7 + h < 15:
                    load_wo(h - 5)
            for m in range(3, KC):
                load_wo(m)
            load_ffn(1)

            for i in range(NB * T // P):
                sp.wait_ge(y_act, i + 1)
                sp.wait_ge(y_dve, i + 1)
                dst = (y_prompt, y_sample)[i // 4][0]
                r = (i % 4) * P
                sp.dma_start(dst[r:r + P, :], yout[:, i, :]).then_inc(y_out, 16)
            sp.wait_ge(y_out, 16 * (NB * T // P))

        SEQ_AB = [(c, b) for b in range(NB) for c in range(KC)]
        SEQ_MIX = [(c, b) for c in range(KC) for b in range(NB)]
        SEQ = (SEQ_AB, SEQ_AB, SEQ_AB, SEQ_MIX)
        SEQ = {0: SEQ_AB, 1: SEQ_AB, 2: SEQ_AB, 3: SEQ_MIX}
        GAIN = {0: V_MIX, 1: V_FFN, 2: V_MIX + KC, 3: V_FFN + KC}

        def acc_index(k, r):
            return 14 * k + sum(1 for c, _ in SEQ[k][:r + 1] if c > 0)

        @block.tensor
        def _(pe):
            def product(out, parts, first, last, done=None):
                n = len(parts)
                for i, (w, m) in enumerate(parts):
                    ins = pe.matmul(out, w, m, start=first and i == 0, stop=last and i == n - 1)
                if done is not None:
                    ins.then_inc(done, 1)

            def three(whi, wlo, mhi, mlo):
                return [(whi, mhi), (whi, mlo), (wlo, mhi)]

            def w_chunk(u, k):
                return w_hi_t[:, slot(u), k * P:(k + 1) * P], w_lo_t[:, slot(u), k * P:(k + 1) * P]

            def mean_square(k, b, out):
                r = max(i for i, (_, bb) in enumerate(SEQ[k]) if bb == b)
                pe.wait_ge(n_acc, acc_index(k, r))
                pe.matmul(out[:, :], ones[:, :], stat[b][:, :], start=True, stop=True).then_inc(n_ms, 1)

            pe.wait_ge(ident_made, 2)
            pe.wait_ge(vec_landed, 6 * 16)
            pe.transpose(bank[0][:, 0:N_VEC], vec_in[:, :], ident[0:N_VEC, 0:N_VEC]).then_inc(vec_turned, 1)
            for q in range(2 * NB * T // P):
                i, half = q // 2, q % 2
                if half == 0:
                    pe.wait_ge(x_in[i], 16)
                if q >= 4:
                    if q % 2 == 0:
                        pe.wait_ge(x_copied_act, q // 2 - 1)
                    else:
                        pe.wait_ge(x_copied_dve, q // 2 - 1)
                for c in range(4):
                    ins = pe.transpose(b_down[q % 4][:, c * P:(c + 1) * P],
                                       xin[:, i, (4 * half + c) * P:(4 * half + c + 1) * P], ident[:, :])
                ins.then_inc(x_turned, 1)
            pe.wait_ge(ones_made, 1)
            mean_square(0, 0, bank[1])
            mean_square(0, 1, bank[2])

            for b in range(NB):
                for g in range(4):
                    pe.wait_ge(w_lo, g // 2 + 1)
                    pe.wait_ge(m_lo, KC * b + 2 * g + 2)
                    for m in range(2):
                        q = KC * b + 2 * g + m
                        if q >= 4:
                            pe.wait_ge(m_scaled, q - 3)
                        elif q == 0:
                            pe.wait_ge(x_copied_act, 8)
                            pe.wait_ge(x_copied_dve, 8)
                        parts = []
                        for k in range(2):
                            lo = (g % 2) * 512 + k * 256 + m * P
                            s = slot(g // 2)
                            parts += three(w_hi_t[:, s, lo:lo + P], w_lo_t[:, s, lo:lo + P],
                                           h_hi[:, 2 * g + k, tok(b)], h_lo[:, 2 * g + k, tok(b)])
                        product(b_down[q % 4][:, :], parts, True, True, m_filled)

            def gate_up_half(layer, g, c, b, up, t, norm=None, n=None):
                u = gu_unit(layer, g, c, up)
                parts = []
                out = (b_up if up else b_gate)[t % 2]
                for k in range(KC):
                    whi, wlo = w_chunk(u, k)
                    parts = three(whi, wlo, h_hi[:, k, tok(b)], h_lo[:, k, tok(b)])
                    if norm is not None:
                        pe.wait_ge(n_lo, (norm - 1) * 16 + KC * b + k + 1)
                    product(out[:, :], parts, k == 0, k == KC - 1,
                            None if k < KC - 1 else (up_done if up else gate_done))

            def tile(layer, g, t, j=None, norm=None, between=None):
                c, b = t % 2, t // 2
                n = N_TILE * layer + 4 * g + t
                step = 0 if j is None else j * (4 * BODIES)
                ustep = 0 if j is None else j * (6 * BODIES)
                if 4 * g + t >= 2:
                    pe.wait_ge(prod_done, step + n - 1)
                for up in range(2):
                    if b == 0:
                        pe.wait_ge(w_lo, ustep + gu_unit(layer, g, c, up) + 1)
                    gate_up_half(layer, g, c, b, up, t, norm if up == 0 and c == 0 else None)
                    if between is not None and up == 0:
                        between()

            def down_bank(layer, g, b, m, j=None):
                i = KC * b + m
                q = N_DOWN * layer + 16 * g + i
                step = 0 if j is None else j * (16 * BODIES)
                if 16 * g + i >= 4:
                    pe.wait_ge(down_added, step + q - 3)
                parts = []
                for c in range(GF):
                    whi, wlo = w_chunk(down_unit(layer, g, c), m)
                    parts += three(whi, wlo, act_hi[:, g % 2, c, tok(b)], act_lo[:, g % 2, c, tok(b)])
                product(b_down[i % 4][:, :], parts, True, True, down_filled)

            def down(layer, g, j=None):
                tstep = 0 if j is None else j * (4 * BODIES)
                ustep = 0 if j is None else j * (6 * BODIES)
                pe.wait_ge(w_lo, ustep + down_unit(layer, g, 1) + 1)
                pe.wait_ge(act_lo_done, tstep + N_TILE * layer + 4 * (g + 1))
                for b in range(NB):
                    for m in range(KC):
                        down_bank(layer, g, b, m, j)

            def swiglu(layer, norm, ms_b1):
                for t in range(4):
                    tile(layer, 0, t, norm=norm, between=ms_b1 if t == 0 else None)
                with pe.Fori(0, LOOPS) as j:
                    for g in range(1, 1 + BODIES):
                        for t in range(4):
                            tile(layer, g, t, j)
                        down(layer, g - 1, j)
                for g in range(FIRST_PEELED, NG):
                    for t in range(4):
                        tile(layer, g, t)
                    down(layer, g - 1)

            def down_last(layer, inside):
                g = NG - 1
                pe.wait_ge(w_lo, down_unit(layer, g, 1) + 1)
                pe.wait_ge(act_lo_done, N_TILE * (layer + 1))
                for b in range(NB):
                    for m in range(KC):
                        down_bank(layer, g, b, m)
                        if b == 1 and m == 2 and inside is not None:
                            inside()

            mean_square(1, 0, bank[3])
            swiglu(0, 1, lambda: mean_square(1, 1, b_down[0]))
            down_last(0, lambda: mean_square(2, 0, bank[1]))

            def project(idx, u):
                b = idx % 2
                if idx >= 2:
                    pe.wait_ge(p_gain, idx - 1)
                if b == 0:
                    pe.wait_ge(w_lo, u + 1)
                for k in range(KC):
                    whi, wlo = w_chunk(u, k)
                    if idx < 2:
                        pe.wait_ge(n_lo, 16 + KC * b + k + 1)
                    product(b_gate[b][:, :], three(whi, wlo, h_hi[:, k, tok(b)], h_lo[:, k, tok(b)]),
                            k == 0, k == KC - 1, proj_done if k == KC - 1 else None)

            def head_square(idx):
                pe.wait_ge(p_sq, idx + 1)
                if idx >= 2:
                    pe.wait_ge(p_sqrt, idx - 1)
                pe.matmul(b_up[idx % 2][:, :], ones[:, :], qsq[idx % 2][:, :], start=True,
                          stop=True).then_inc(p_ms, 1)

            project(0, U_QKV)
            mean_square(2, 1, b_down[0])
            project(1, U_QKV)
            head_square(0)
            project(2, U_QKV + 1)
            head_square(1)
            project(3, U_QKV + 1)
            head_square(2)
            pe.wait_ge(w_lo, U_QKV + 4)
            for t in range(NB * T // P):
                if t >= 4:
                    pe.wait_ge(v_lo_done, t - 3)
                parts = []
                for k in range(KC):
                    s = slot(U_QKV + 2 + k // 4)
                    c0 = (k % 4) * 256
                    hh, hl = h_hi[:, k, t * P:(t + 1) * P], h_lo[:, k, t * P:(t + 1) * P]
                    wh, wl = w_hi_t[:, s, c0:c0 + 256], w_lo_t[:, s, c0:c0 + 256]
                    parts += [(hh, wh), (hh, wl), (hl, wh)]
                product(b_down[t % 4][:, 0:256], parts, True, True, v_filled)
                if t == 0:
                    head_square(3)
            for i in range(2 * HEADS):
                project(4 + i, U_QKV + 4 + i // 2)
                if i >= 1:
                    head_square(3 + i)
            head_square(3 + 2 * HEADS)

            def scores(a):
                b, kv = a // 8, a % 8 // 4
                pe.wait_ge(a_q, a + 1)
                for i in range(4):
                    s = 4 * a + i
                    if s >= 3:
                        pe.wait_ge(a_exp, s - 2)
                    c = slice(i * P, (i + 1) * P)
                    product(bank[s % 3][:, :],
                            three(qs_hi[:, a % 2, c], qs_lo[:, a % 2, c], k_hi[:, kv, tok(b)], k_lo[:, kv, tok(b)]),
                            True, True, s_filled)

            def turn_probs(a):
                if a >= 1:
                    pe.wait_ge(a_ptlo, 4 * a)
                else:
                    pe.wait_ge(v_lo_done, 8)
                for i in range(4):
                    pe.wait_ge(a_prob, 4 * a + i + 1)
                    for sc in range(4):
                        ins = pe.transpose(b_down[sc][:, i * P:(i + 1) * P], prob[:, i, sc * P:(sc + 1) * P],
                                           ident[:, :])
                        if i == 3:
                            ins.then_inc(pt_filled, 1)

            def attend(a):
                b, kv = a // 8, a % 8 // 4
                if a >= 1:
                    pe.wait_ge(o_copied, a)
                for sc in range(4):
                    pe.wait_ge(a_ptlo, 4 * a + sc + 1)
                    t, c = 4 * b + sc, slice(kv * HD, (kv + 1) * HD)
                    product(bank[3][:, :], three(v_hi[:, t, c], v_lo[:, t, c], pt_hi[:, sc, :], pt_lo[:, sc, :]),
                            sc == 0, sc == 3, o_filled if sc == 3 else None)

            pe.wait_ge(p_sqrt, 20)
            pe.wait_ge(p_gain, 20)
            scores(0)
            for a in range(16):
                turn_probs(a)
                if a + 1 < 16:
                    scores(a + 1)
                attend(a)

            for m in range(KC):
                pe.wait_ge(w_lo, U_WO + m + 1)
                for b in range(NB):
                    w = 2 * m + b
                    if w >= 4:
                        pe.wait_ge(wo_added, w - 3)
                    if m == 0 and b == 0:
                        pe.wait_ge(o0_split, 8)
                    for k in range(HEADS):
                        if m == 0 and b == 1:
                            pe.wait_ge(o1_split, k + 1)
                        whi, wlo = w_chunk(U_WO + m, k)
                        product(b_down[w % 4][:, :], three(whi, wlo, o_hi[b][:, k, :], o_lo[b][:, k, :]),
                                k == 0, k == HEADS - 1, wo_filled if k == HEADS - 1 else None)
            mean_square(3, 0, bank[1])
            swiglu(1, 3, lambda: mean_square(3, 1, b_down[0]))
            down_last(1, None)

            for q in range(2 * NB * T // P):
                i, half = q // 2, q % 2
                if q % 8 == 0:
                    pe.wait_ge(down_added, N_DOWN * 2 - 8 + q)
                if q >= 4:
                    if half == 0:
                        pe.wait_ge(y_act, q // 2 - 1)
                    else:
                        pe.wait_ge(y_dve, q // 2 - 1)
                for c in range(4):
                    ins = pe.transpose(bank[q % 4][:, c * P:(c + 1) * P],
                                       x[:, 4 * half + c, i * P:(i + 1) * P], ident[:, :])
                ins.then_inc(y_turned, 1)

        @block.scalar
        def _(act):
            def split_hi(u, step=None):
                if step is None:
                    act.wait_ge(raw_in[u % RAW], 16 * (u // RAW + 1))
                else:
                    act.wait_ge(raw_in[u % RAW], step * (16 * 6 * BODIES // RAW) + 16 * (u // RAW + 1))
                nc.scalar.copy(w_hi_t[:, slot(u), :], raw[:, u % RAW, :]).then_inc(w_hi, 1)

            def square(k, r, ready):
                c, b = SEQ[k][r]
                ready(c, b)
                if c == 0:
                    dst = stat[b]
                else:
                    i = acc_index(k, r)
                    if i % 14 != 1 and i > 2 or k > 0:
                        act.wait_ge(n_acc, i - 2)
                    dst = sqr[i % 2]
                nc.scalar.activation(dst[:, :], x[:, c, tok(b)], ACT.Square).then_inc(n_sq, 1)

            def root(k, b, src):
                act.wait_ge(n_ms, 2 * k + b + 1)
                nc.scalar.activation(stat[b][:, :], src[:, :], ACT.Sqrt, bias=epst[:, 0:1],
                                     scale=1.0 / D).then_inc(n_sqrt, 1)

            def norm_hi(k, b, c):
                i = 16 * (k - 1) + KC * b + c
                act.wait_ge(n_full, i + 1)
                nc.scalar.copy(h_hi[:, c, tok(b)], full[i % 2][:, :]).then_inc(n_hi, 1)

            for i in range(NB * T // P):
                act.wait_ge(x_turned, 2 * i + 1)
                nc.scalar.copy(x[:, 0:4, i * P:(i + 1) * P],
                               b_down[(2 * i) % 4][:, :].rearrange("p (c t) -> p c t", c=4)).then_inc(x_copied_act, 1)
            act.wait_ge(x_turned, 16)

            def x_here(c, b):
                act.wait_ge(x_copied_act, 4 * (b + 1))
                act.wait_ge(x_copied_dve, 4 * (b + 1))

            act.wait_ge(eps_made, 2)
            for r in range(8):
                square(0, r, x_here)
            root(0, 0, bank[1])
            split_hi(0)
            split_hi(1)
            for r in range(8, 16):
                square(0, r, x_here)
            root(0, 1, bank[2])

            def scaled(q):
                c = q % KC
                act.wait_ge(m_filled, q + 1)
                if q >= 2:
                    act.wait_ge(m_x, q - 1)
                else:
                    act.wait_ge(vec_ready, 2)
                nc.scalar.activation(silu_t[q % 2][:, :], b_down[q % 4][:, :], ACT.Identity,
                                     bias=vec[:, V_BS + c:V_BS + c + 1],
                                     scale=vec[:, V_PS + c:V_PS + c + 1]).then_inc(m_scaled, 1)

            def x_mixed(c, b):
                act.wait_ge(m_x, KC * b + c + 1)
                if c == 0:
                    act.wait_ge(m_row, KC * (b + 1))

            for i in range(16):
                b, c = i // KC, i % KC
                act.wait_ge(m_full, i + 1)
                nc.scalar.copy(h_hi[:, c, tok(b)], full[i % 2][:, :]).then_inc(m_hi, 1)
                if 4 <= i < 14 and i % 2 == 1:
                    scaled(i - 5)
                    scaled(i - 4)
            for r in range(8):
                square(1, r, x_mixed)
            for q in range(10, 16):
                scaled(q)
            for i in range(4):
                split_hi(U_FFN0 + i)
            act.wait_ge(m_filled, 16)
            root(1, 0, bank[3])
            for c in range(KC):
                square(1, 8 + c, x_mixed)
                norm_hi(1, 0, c)
            for i in range(4, 6):
                split_hi(U_FFN0 + i)
            root(1, 1, b_down[0])
            for c in range(KC):
                norm_hi(1, 1, c)

            def silu(layer, g, t, j=None):
                i = 4 * g + t
                n = N_TILE * layer + i
                step = 0 if j is None else j * (4 * BODIES)
                act.wait_ge(gate_done, step + n + 1)
                if i >= 2:
                    act.wait_ge(prod_done, step + n - 1)
                nc.scalar.activation(silu_t[t % 2][:, :], b_gate[t % 2][:, :], ACT.Silu).then_inc(silu_done, 1)

            def hidden_hi(layer, g, t, j=None):
                c, b = t % 2, t // 2
                step = 0 if j is None else j * (4 * BODIES)
                act.wait_ge(prod_done, step + N_TILE * layer + 4 * g + t + 1)
                nc.scalar.copy(act_hi[:, g % 2, c, tok(b)], full[t % 2][:, :]).then_inc(act_hi_done, 1)

            def group(layer, g, j=None):
                tstep = 0 if j is None else j * (4 * BODIES)
                dstep = 0 if j is None else j * (16 * BODIES)
                for t in range(4):
                    silu(layer, g, t, j)
                    hidden_hi(layer, g, t, j)
                    if t >= 2:
                        act.wait_ge(up_done, tstep + N_TILE * layer + 4 * g + t + 1)
                        for up in range(2):
                            u = gu_unit(layer, g, t - 2, up) + RING
                            if u < U_FFN[layer] + N_FFN or (layer == 0 and slot(u) < 2):
                                split_hi(u, j)
                if g >= 1 and down_unit(layer, g - 1, 0) + RING < U_FFN[layer] + N_FFN:
                    act.wait_ge(down_filled, dstep + N_DOWN * layer + 16 * g)
                    for c in range(GF):
                        split_hi(down_unit(layer, g - 1, c) + RING, j)

            def swiglu(layer):
                group(layer, 0)
                with act.Fori(0, LOOPS) as j:
                    for g in range(1, 1 + BODIES):
                        group(layer, g, j)
                for g in range(FIRST_PEELED, NG):
                    group(layer, g)

            swiglu(0)

            def x_ffn0(c, b):
                act.wait_ge(down_added, N_DOWN - 16 + KC * b + c + 1)

            for r in range(8):
                square(2, r, x_ffn0)
            root(2, 0, bank[1])
            for c in range(KC):
                square(2, 8 + c, x_ffn0)
                norm_hi(2, 0, c)
            root(2, 1, b_down[0])
            for c in range(KC):
                norm_hi(2, 1, c)

            def gain(idx):
                b = idx % 2
                act.wait_ge(proj_done, idx + 1)
                if idx >= 2:
                    act.wait_ge(p_done, idx - 1)
                g = V_KG if idx < 4 else V_QG
                nc.scalar.activation(qsq[b][:, :], b_gate[b][:, :], ACT.Square).then_inc(p_sq, 1)
                nc.scalar.activation(qg[b][:, :], b_gate[b][:, :], ACT.Copy,
                                     scale=vec[:, g:g + 1]).then_inc(p_gain, 1)

            def head_root(idx):
                act.wait_ge(p_ms, idx + 1)
                key = idx < 4
                nc.scalar.activation(qsq[idx % 2][:, :], b_up[idx % 2][:, :], ACT.Sqrt,
                                     bias=epst[:, 0:1] if key else epst[:, 1:2],
                                     scale=1.0 / HD if key else 1.0).then_inc(p_sqrt, 1)

            def key_hi(idx):
                act.wait_ge(p_fin, idx + 1)
                nc.scalar.copy(k_hi[:, idx // 2, tok(idx % 2)], rot[idx % 2][:, :]).then_inc(p_hi, 1)

            gain(0)
            gain(1)
            split_hi(U_QKV + 2)
            for idx in range(2):
                head_root(idx)
                key_hi(idx)
                gain(idx + 2)
            split_hi(U_QKV + 3)
            for t in range(NB * T // P):
                act.wait_ge(v_filled, t + 1)
                nc.scalar.copy(v_hi[:, t, :], b_down[t % 4][:, 0:256]).then_inc(v_hi_done, 1)
                if t in (1, 3):
                    idx = 2 + t // 2
                    head_root(idx)
                    key_hi(idx)
            split_hi(U_QKV + 4)
            split_hi(U_QKV + 5)
            for idx in range(4, 20):
                gain(idx)
                if idx >= 5:
                    head_root(idx - 1)
                if idx % 2 == 1:
                    split_hi(U_QKV + 4 + (idx - 5) // 2 + 2)
            head_root(19)

            def exps(a):
                for i in range(4):
                    s = 4 * a + i
                    act.wait_ge(a_max, s + 1)
                    if a >= 1:
                        act.wait_ge(pt_filled, 4 * a)
                    nc.scalar.activation(prob[:, i, :], bank[s % 3][:, :], ACT.Exp, bias=nmax[:, s % 8:s % 8 + 1],
                                         accum_out=rsum[:, s % 8:s % 8 + 1]).then_inc(a_exp, 1)

            exps(0)
            for a in range(16):
                for sc in range(4):
                    act.wait_ge(pt_filled, 4 * a + sc + 1)
                    if a >= 1:
                        act.wait_ge(o_filled, a)
                    nc.scalar.copy(pt_hi[:, sc, :], b_down[sc][:, :]).then_inc(a_pthi, 1)
                if a + 1 < 16:
                    exps(a + 1)
                act.wait_ge(o_filled, a + 1)
                nc.scalar.copy(q_of(a % 8, a // 8), bank[3][:, :]).then_inc(o_copied, 1)
            act.wait_ge(o_copied, 16)
            for h in range(HEADS):
                nc.scalar.copy(o_hi[1][:, h, :], q_of(h, 1)).then_inc(o1_hi, 1)

            def x_attn(c, b):
                act.wait_ge(wo_added, 2 * c + b + 1)

            for m in range(KC):
                if m >= 1:
                    act.wait_ge(wo_filled, 2 * m)
                    u = U_WO + m + 1
                    if u < U_FFN1:
                        split_hi(u)
                    square(3, 2 * (m - 1), x_attn)
                    square(3, 2 * (m - 1) + 1, x_attn)
            split_hi(U_FFN1)
            act.wait_ge(o0_split, 8)
            act.wait_ge(o1_split, 8)
            for i in range(2, RING):
                if i == 2:
                    act.wait_ge(wo_filled, 16)
                    split_hi(U_FFN1 + 1)
                split_hi(U_FFN1 + i)
            square(3, 14, x_attn)
            square(3, 15, x_attn)
            root(3, 0, bank[1])
            for c in range(KC):
                norm_hi(3, 0, c)
            root(3, 1, b_down[0])
            for c in range(KC):
                norm_hi(3, 1, c)
            swiglu(1)

            for i in range(NB * T // P):
                act.wait_ge(y_turned, 2 * i + 1)
                nc.scalar.copy(yout[:, i, 0:512], bank[(2 * i) % 4][:, :]).then_inc(y_act, 1)

        @block.vector
        def _(dve):
            def split_lo(u, step=None):
                dve.wait_ge(w_hi, u + 1 if step is None else step * (6 * BODIES) + u + 1)
                nc.vector.tensor_tensor(w_lo_t[:, slot(u), :], raw[:, u % RAW, :],
                                        w_hi_t[:, slot(u), :].bitcast(F32), ALU.subtract).then_inc(w_lo, 1)

            def inverse(k, b):
                dve.wait_ge(n_sqrt, 2 * k + b + 1)
                nc.vector.reciprocal(stat[b][:, :], stat[b][:, :]).then_inc(n_rstd, 1)

            def norm_full(k, b, c):
                i = 16 * (k - 1) + KC * b + c
                dve.wait_ge(n_rstd, 2 * k + b + 1)
                if i >= 2:
                    dve.wait_ge(n_lo, i - 1)
                g = GAIN[k] + c
                nc.vector.scalar_tensor_tensor(full[i % 2][:, :], x[:, c, tok(b)], vec[:, g:g + 1], stat[b][:, :],
                                               ALU.mult, ALU.mult).then_inc(n_full, 1)

            def norm_lo(k, b, c):
                i = 16 * (k - 1) + KC * b + c
                dve.wait_ge(n_hi, i + 1)
                nc.vector.tensor_tensor(h_lo[:, c, tok(b)], full[i % 2][:, :], h_hi[:, c, tok(b)].bitcast(F32),
                                        ALU.subtract).then_inc(n_lo, 1)

            def norm_batch(k, b, before=None):
                inverse(k, b)
                for c in range(KC):
                    if before is not None:
                        before(c)
                    norm_full(k, b, c)
                    if c >= 1:
                        norm_lo(k, b, c - 1)
                norm_lo(k, b, KC - 1)

            dve.wait_ge(vec_turned, 1)
            nc.vector.tensor_copy(vec[:, 0:N_VEC], bank[0][:, 0:N_VEC]).then_inc(vec_ready, 1)
            dve.wait_ge(vec_ready, 1)
            nc.vector.tensor_tensor(vec[:, V_BS:V_BS + KC], vec[:, V_PB:V_PB + KC], vec[:, V_PS:V_PS + KC],
                                    ALU.mult).then_inc(vec_ready, 1)
            for i in range(NB * T // P):
                dve.wait_ge(x_turned, 2 * i + 2)
                nc.vector.tensor_copy(x[:, 4:8, i * P:(i + 1) * P],
                                      b_down[(2 * i + 1) % 4][:, :].rearrange("p (c t) -> p c t", c=4)
                                      ).then_inc(x_copied_dve, 1)

            steps = [0]

            def chain(ins):
                steps[0] += 1
                ins.then_inc(m_step, 1)
                dve.wait_ge(m_step, steps[0])

            def row(b, c):
                i = KC * b + c
                if i >= 4:
                    dve.wait_ge(m_full, i - 3)
                nc.vector.scalar_tensor_tensor(hp[i % 4][:, PAD:PAD + T], x[:, c, tok(b)],
                                               vec[:, V_MIX + c:V_MIX + c + 1], stat[b][:, :],
                                               ALU.mult, ALU.mult).then_inc(m_row, 1)

            def pooled(b, c, win):
                i = KC * b + c
                ends = win[:, PAD:PAD + T].rearrange("p (n e) -> p n e", e=EDGE)[:, 0:T // EDGE:T // EDGE - 1, :]
                chain(nc.vector.tensor_tensor(ends, ends, edge[:, c // 2, :, :], ALU.mult))
                if i >= 2:
                    dve.wait_ge(m_lo, i - 1)
                nc.vector.scalar_tensor_tensor(full[i % 2][:, :], win[:, PAD:PAD + T], 1.0 / WINDOWS[c // 2],
                                               hp[i % 4][:, PAD:PAD + T], ALU.mult, ALU.subtract
                                               ).then_inc(m_full, 1)

            def pooled_lo(b, c):
                i = KC * b + c
                dve.wait_ge(m_hi, i + 1)
                nc.vector.tensor_tensor(h_lo[:, c, tok(b)], full[i % 2][:, :], h_hi[:, c, tok(b)].bitcast(F32),
                                        ALU.subtract).then_inc(m_lo, 1)

            dve.wait_ge(pads_made, 4)
            dve.wait_ge(edge_landed, 16)
            for b in range(NB):
                inverse(0, b)
                dve.wait_ge(n_rstd, b + 1)
                if b == 0:
                    split_lo(0)
                    split_lo(1)
                for pair in range(4):
                    even, odd = 2 * pair, 2 * pair + 1
                    row(b, odd)
                    row(b, even)
                    dve.wait_ge(m_row, KC * b + 2 * pair + 2)
                    if pair >= 1:
                        dve.wait_ge(m_psum, 4 * b + pair)
                        pooled(b, odd - 2, wsum_pool[2 * (pair - 1) % 4 + (pair - 1) % 2])
                        pooled_lo(b, odd - 2)
                    elif b >= 1:
                        dve.wait_ge(m_lo, KC)
                    win = window_sums(nc.vector, hp[(KC * b + even) % 4], wsum, pair + 1, chain)
                    pooled(b, even, win)
                    pooled_lo(b, even)
                dve.wait_ge(m_psum, 4 * b + 4)
                pooled(b, KC - 1, wsum_pool[2 * 3 % 4 + 3 % 2])
                pooled_lo(b, KC - 1)

            for i in range(4):
                split_lo(U_FFN0 + i)
            norm_batch(1, 0)
            for i in range(4, 6):
                split_lo(U_FFN0 + i)
            norm_batch(1, 1)

            def hidden(layer, g, t, j=None):
                c, b = t % 2, t // 2
                i = 4 * g + t
                n = N_TILE * layer + i
                step = 0 if j is None else j * (4 * BODIES)
                dve.wait_ge(silu_done, step + n + 1)
                dve.wait_ge(up_done, step + n + 1)
                if i >= 2:
                    dve.wait_ge(act_lo_done, step + n - 1)
                else:
                    dve.wait_ge(n_lo, 16 if layer == 0 else 48)
                nc.vector.tensor_tensor(full[t % 2][:, :], silu_t[t % 2][:, :], b_up[t % 2][:, :],
                                        ALU.mult).then_inc(prod_done, 1)
                dve.wait_ge(act_hi_done, step + n + 1)
                nc.vector.tensor_tensor(act_lo[:, g % 2, c, tok(b)], full[t % 2][:, :],
                                        act_hi[:, g % 2, c, tok(b)].bitcast(F32), ALU.subtract
                                        ).then_inc(act_lo_done, 1)

            def add_down(layer, g, i, j=None):
                q = N_DOWN * layer + 16 * g + i
                step = 0 if j is None else j * (16 * BODIES)
                dve.wait_ge(down_filled, step + q + 1)
                xc = x[:, i % KC, tok(i // KC)]
                nc.vector.tensor_tensor(xc, b_down[i % 4][:, :], xc, ALU.add).then_inc(down_added, 1)

            def group(layer, g, j=None):
                for t in range(4):
                    hidden(layer, g, t, j)
                    if t >= 2:
                        for up in range(2):
                            u = gu_unit(layer, g, t - 2, up) + RING
                            if u < U_FFN[layer] + N_FFN or (layer == 0 and slot(u) < 2):
                                split_lo(u, j)
                if g >= 1:
                    for i in range(16):
                        add_down(layer, g - 1, i, j)
                    if down_unit(layer, g - 1, 0) + RING < U_FFN[layer] + N_FFN:
                        for c in range(GF):
                            split_lo(down_unit(layer, g - 1, c) + RING, j)

            def swiglu(layer):
                group(layer, 0)
                with dve.Fori(0, LOOPS) as j:
                    for g in range(1, 1 + BODIES):
                        group(layer, g, j)
                for g in range(FIRST_PEELED, NG):
                    group(layer, g)

            swiglu(0)
            for i in range(KC):
                add_down(0, NG - 1, i)
            norm_batch(2, 0, before=lambda c: add_down(0, NG - 1, KC + c))
            norm_batch(2, 1)

            def rope(idx):
                b = idx % 2
                dve.wait_ge(p_sqrt, idx + 1)
                nc.vector.reciprocal(qsq[b][:, :], qsq[b][:, :]).then_inc(p_r, 1)
                dve.wait_ge(rot_in[b], 64 * (idx // 2 + 1))
                dve.wait_ge(tables_in, 32)
                nc.vector.tensor_tensor(rot[b][:, :], rot[b][:, :], sin_t[:, :], ALU.mult).then_inc(p_sin, 1)
                dve.wait_ge(p_cos, idx + 1)
                dve.wait_ge(p_sin, idx + 1)
                nc.vector.tensor_tensor(qg[b][:, :], qg[b][:, :], rot[b][:, :], ALU.add).then_inc(p_sum, 1)
                dve.wait_ge(p_sum, idx + 1)
                dve.wait_ge(p_r, idx + 1)
                if idx < 4:
                    nc.vector.tensor_tensor(rot[b][:, :], qg[b][:, :], qsq[b][:, :], ALU.mult).then_inc(p_fin, 1)
                    dve.wait_ge(p_hi, idx + 1)
                    nc.vector.tensor_tensor(k_lo[:, idx // 2, tok(b)], rot[b][:, :],
                                            k_hi[:, idx // 2, tok(b)].bitcast(F32), ALU.subtract
                                            ).then_inc(p_done, 1)
                else:
                    nc.vector.tensor_tensor(q_of((idx - 4) // 2, b), qg[b][:, :], qsq[b][:, :],
                                            ALU.mult).then_inc(p_done, 1)

            split_lo(U_QKV + 2)
            rope(0)
            rope(1)
            split_lo(U_QKV + 3)
            for t in range(NB * T // P):
                dve.wait_ge(v_hi_done, t + 1)
                nc.vector.tensor_tensor(v_lo[:, t, :], b_down[t % 4][:, 0:256], v_hi[:, t, :].bitcast(F32),
                                        ALU.subtract).then_inc(v_lo_done, 1)
                if t in (1, 3):
                    rope(2 + t // 2)
            split_lo(U_QKV + 4)
            split_lo(U_QKV + 5)
            for idx in range(4, 20):
                if idx >= 5:
                    rope(idx - 1)
                if idx % 2 == 1:
                    split_lo(U_QKV + 4 + (idx - 5) // 2 + 2)
            rope(19)

            def row_max(s):
                dve.wait_ge(s_filled, s + 1)
                if s >= 8:
                    dve.wait_ge(a_prob, s - 7)
                nc.vector.tensor_reduce(nmax[:, s % 8:s % 8 + 1], bank[s % 3][:, :], AX.X, ALU.max,
                                        negate=True).then_inc(a_max, 1)

            def normalise(s):
                dve.wait_ge(a_exp, s + 1)
                col = slice(s % 8, s % 8 + 1)
                nc.vector.reciprocal(rinv[:, col], rsum[:, col]).then_inc(a_rinv, 1)
                dve.wait_ge(a_rinv, s + 1)
                nc.vector.tensor_scalar(prob[:, s % 4, :], prob[:, s % 4, :], rinv[:, col], None,
                                        ALU.mult).then_inc(a_prob, 1)

            def softmax(a):
                row_max(4 * a)
                for i in range(1, 4):
                    row_max(4 * a + i)
                    normalise(4 * a + i - 1)
                normalise(4 * a + 3)

            softmax(0)
            for a in range(16):
                for sc in range(4):
                    dve.wait_ge(a_pthi, 4 * a + sc + 1)
                    nc.vector.tensor_tensor(pt_lo[:, sc, :], b_down[sc][:, :], pt_hi[:, sc, :].bitcast(F32),
                                            ALU.subtract).then_inc(a_ptlo, 1)
                if a + 1 < 16:
                    softmax(a + 1)
            for h in range(HEADS):
                dve.wait_ge(o1_hi, h + 1)
                nc.vector.tensor_tensor(o_lo[1][:, h, :], q_of(h, 1), o_hi[1][:, h, :].bitcast(F32),
                                        ALU.subtract).then_inc(o1_split, 1)

            def add_wo(w):
                dve.wait_ge(wo_filled, w + 1)
                xc = x[:, w // 2, tok(w % 2)]
                nc.vector.tensor_tensor(xc, b_down[w % 4][:, :], xc, ALU.add).then_inc(wo_added, 1)

            for m in range(KC):
                if m >= 1 and U_WO + m + 1 < U_FFN1:
                    split_lo(U_WO + m + 1)
                add_wo(2 * m)
                add_wo(2 * m + 1)
            for i in range(RING):
                split_lo(U_FFN1 + i)
            norm_batch(3, 0)
            norm_batch(3, 1)
            swiglu(1)
            for i in range(16):
                add_down(1, NG - 1, i)

            for i in range(NB * T // P):
                dve.wait_ge(y_turned, 2 * i + 2)
                nc.vector.tensor_copy(yout[:, i, 512:1024], bank[(2 * i + 1) % 4][:, :]).then_inc(y_dve, 1)

        @block.gpsimd
        def _(pool):
            nc.gpsimd.memset(ident[:, :], 0.0).then_inc(ident_made, 1)
            pool.wait_ge(ident_made, 1)
            nc.gpsimd.affine_select(out=ident[:, :], in_=ident[:, :], compare_op=ALU.not_equal, fill=1.0,
                                    base=0, pattern=[[-1, P]], channel_multiplier=1).then_inc(ident_made, 1)
            nc.gpsimd.memset(ones[:, :], 1.0).then_inc(ones_made, 1)
            nc.gpsimd.memset(epst[:, 0:1], EPS).then_inc(eps_made, 1)
            nc.gpsimd.memset(epst[:, 1:2], EPS * HD).then_inc(eps_made, 1)
            for i in range(4):
                nc.gpsimd.memset(hp[i][:, :], 0.0).then_inc(pads_made, 1)

            def add_squares(k, r):
                c, b = SEQ[k][r]
                if c == 0:
                    return
                i = acc_index(k, r)
                pool.wait_ge(n_sq, 16 * k + r + 1)
                if i >= 2:
                    pool.wait_ge(n_acc, i - 1)
                nc.gpsimd.tensor_tensor(out=stat[b][:, :], in0=stat[b][:, :], in1=sqr[i % 2][:, :],
                                        op=ALU.add).then_inc(n_acc, 1)

            for r in range(16):
                add_squares(0, r)

            steps = [0]

            def chain(ins):
                steps[0] += 1
                ins.then_inc(m_pstep, 1)
                pool.wait_ge(m_pstep, steps[0])

            def add_mixed(q):
                b, c = q // KC, q % KC
                pool.wait_ge(m_scaled, q + 1)
                nc.gpsimd.tensor_tensor(out=x[:, c, tok(b)], in0=x[:, c, tok(b)], in1=silu_t[q % 2][:, :],
                                        op=ALU.add).then_inc(m_x, 1)

            for b in range(NB):
                for pair in range(4):
                    i = 4 * b + pair
                    pool.wait_ge(m_row, 2 * i + 1)
                    if i >= 2:
                        pool.wait_ge(m_full, 2 * (i - 2) + 2)
                    bufs = wsum_pool[2 * (pair % 2):2 * (pair % 2) + 2]
                    window_sums(nc.gpsimd, hp[(KC * b + 2 * pair + 1) % 4], bufs, pair + 1, chain,
                                final=lambda ins: ins.then_inc(m_psum, 1))
                    if b == 1:
                        add_mixed(2 * pair)
                        add_mixed(2 * pair + 1)
            for r in range(8):
                add_squares(1, r)
            for c in range(KC):
                add_mixed(KC + c)
            for r in range(8, 16):
                add_squares(1, r)
            for r in range(16):
                add_squares(2, r)

            for idx in range(20):
                b = idx % 2
                if idx == 0:
                    pool.wait_ge(tables_in, 32)
                pool.wait_ge(rot_in[b], 64 * (idx // 2 + 1))
                nc.gpsimd.tensor_tensor(out=qg[b][:, :], in0=qg[b][:, :], in1=cos_t[:, :],
                                        op=ALU.mult).then_inc(p_cos, 1)

            def split_q(a):
                pool.wait_ge(p_done, 4 + 2 * (a % 8) + a // 8 + 1)
                if a == 0:
                    pool.wait_ge(proj_done, 20)
                if a >= 2:
                    pool.wait_ge(s_filled, 4 * (a - 1))
                src = q_of(a % 8, a // 8)
                nc.gpsimd.tensor_scalar(qs_hi[:, a % 2, :], src, 1.0, 0.0, ALU.mult, ALU.add).then_inc(a_qhi, 1)
                pool.wait_ge(a_qhi, a + 1)
                nc.gpsimd.tensor_tensor(out=qs_lo[:, a % 2, :], in0=src, in1=qs_hi[:, a % 2, :].bitcast(F32),
                                        op=ALU.subtract).then_inc(a_q, 1)

            split_q(0)
            split_q(1)
            for a in range(16):
                if a + 2 < 16:
                    split_q(a + 2)
                if a < 8:
                    pool.wait_ge(o_copied, a + 1)
                    src = q_of(a, 0)
                    nc.gpsimd.tensor_scalar(o_hi[0][:, a, :], src, 1.0, 0.0, ALU.mult, ALU.add).then_inc(o0_hi, 1)
                    pool.wait_ge(o0_hi, a + 1)
                    nc.gpsimd.tensor_tensor(out=o_lo[0][:, a, :], in0=src, in1=o_hi[0][:, a, :].bitcast(F32),
                                            op=ALU.subtract).then_inc(o0_split, 1)
            for r in range(16):
                add_squares(3, r)


def window_sums(eng, src, bufs, levels, chain, final=None):
    lo, hi, cur = 1, TP, src
    for level in range(levels):
        dst = bufs[level % 2]
        if level == 0:
            a, b = cur[:, 0:TP - 1], cur[:, 1:TP]
        else:
            s = 2 ** (level - 1)
            lo, hi = lo + s, hi - s
            a, b = cur[:, lo - s:hi - s], cur[:, lo + s:hi + s]
        ins = eng.tensor_tensor(out=dst[:, lo:hi], in0=a, in1=b, op=ALU.add)
        if level == levels - 1 and final is not None:
            final(ins)
        else:
            chain(ins)
        cur = dst
    return cur


def tables():
    import numpy as np
    grid_w, axis = 64, HD // 2
    t = np.arange(T)
    inv = (np.float32(10000.0) ** (-np.arange(0, axis, 2, dtype=np.float32) / np.float32(axis))).astype(np.float32)
    cos, sin = np.zeros((HD, T), np.float32), np.zeros((HD, T), np.float32)
    for d in range(HD):
        pos = (t // grid_w if d < axis else t % grid_w).astype(np.float32)
        ang = (pos * inv[d % 32]).astype(np.float32).astype(np.float64)
        cos[d] = np.cos(ang)
        sin[d] = np.sin(ang) * (-1.0 if d % axis < 32 else 1.0)
    edge = np.ones((P, len(WINDOWS), 2, EDGE), np.float32)
    for g, w in enumerate(WINDOWS):
        for side in range(2):
            for e in range(EDGE):
                tt = e if side == 0 else T - EDGE + e
                edge[:, g, side, e] = w / (min(tt + w // 2, T) - max(tt - w // 2, 0))
    return cos, sin, edge


_INS = ["x_prompt", "x_sample", "norm_mix", "norm_ffn", "pool_w", "pool_b", "pool_scale", "attn_w_qkv",
        "attn_q_gain", "attn_k_gain", "attn_w_o", "ffn_w_gate_up", "ffn_w_down"]


def kernel(**inputs):
    import numpy as np
    import concourse.bacc as bacc
    from concourse.bass_utils import run_bass_kernel_spmd as run

    nc = bacc.Bacc("TRN2", target_bir_lowering=False, num_devices=1)
    arrays, args = {}, []
    cos, sin, edge = tables()
    for name, a in [(n, np.ascontiguousarray(inputs[n])) for n in _INS] + [
            ("rope_cos", cos), ("rope_sin", sin), ("edge_tab", edge)]:
        arrays[f"in_{name}"] = a
        args.append(nc.dram_tensor(f"in_{name}", a.shape, mybir.dt.from_np(a.dtype), kind="ExternalInput").ap())
    for name in ("y_prompt", "y_sample"):
        args.append(nc.dram_tensor(f"out_{name}", (1, T, D), F32, kind="ExternalOutput").ap())
    build(nc, *args)
    r = run(nc, [arrays], core_ids=[0])
    return r.results[0]["out_y_prompt"], r.results[0]["out_y_sample"]
```

```python
from contextlib import ExitStack

import concourse.bass as bass
from concourse import mybir

F32 = mybir.dt.float32
F32R = mybir.dt.float32r
ALU = mybir.AluOpType
ACT = mybir.ActivationFunctionType
AX = mybir.AxisListType

P = 128
D = 1024
KC = D // P
T = 512
NB = 2
DFF = 2816
NF = DFF // P
GF = 2
NG = NF // GF
HEADS, KVH, HD = 8, 2, 128
EPS = 1e-6
WINDOWS = (2, 4, 8, 16)
PAD = 8
TP = T + 2 * PAD
EDGE = 8

UNIT = 1024
RAW = 3
RING = 6
U_POOL = 0
U_FFN0 = U_POOL + 2
N_FFN = NG * 3 * GF
N_QKV = 2 * KVH + HEADS
U_QKV = U_FFN0 + N_FFN
U_WO = U_QKV + NB * N_QKV
U_FFN1 = U_WO + NB * KC
U_END = U_FFN1 + N_FFN
U_FFN = (U_FFN0, U_FFN1)
N_TILE = NG * GF * NB
N_DOWN = NG * KC * NB
BODIES = 2
LOOPS = (NG - 2) // BODIES
FIRST_PEELED = 1 + LOOPS * BODIES

N_PROJ = KVH + HEADS
N_PLAIN = N_PROJ + KVH
BESIDE = {-1: ("v", 1), 8: ("s", N_PLAIN + 7)}
BESIDE |= {a: ("p", N_PLAIN + a) for a in range(8)} | {a: ("w", a - 9) for a in range(9, 16)}
RING_WO = 4

V_MIX, V_FFN, V_PB, V_PS, V_QG, V_KG = 0, 16, 32, 40, 48, 49
N_VEC = 50
V_BS = 50


def build(nc, x_prompt, x_sample, norm_mix, norm_ffn, pool_w, pool_b, pool_scale, w_qkv, q_gain,
          k_gain, w_o, w_gu, w_down, rope_cos, rope_sin, edge_tab, y_prompt, y_sample):
    with ExitStack() as ctx:
        base = (nc.sbuf_base + 31) // 32 * 32
        top = [base]

        def at(name, shape, dt, off):
            return nc.alloc_sbuf_tensor_at(name, shape, dt, offset=off)

        def take(nbytes):
            off = top[0]
            top[0] += nbytes
            return off

        o_x, o_h, o_act = take(KC * NB * T * 4), take(KC * NB * T * 8), take(32768)
        o_ring, o_raw, o_tmp = take(RING * UNIT * 8), take(RAW * UNIT * 4), take(8 * T * 4)
        o_const = take(0)
        x = at("x", [P, KC, NB * T], F32, o_x)
        half_hi = [at(f"half_hi{i}", [P, KC, T], F32R, o_h + 32768 * i) for i in range(2)]
        half_lo = [at(f"half_lo{i}", [P, KC, T], F32R, o_h + 32768 * i + 16384) for i in range(2)]
        act_hi = at("act_hi", [P, 2, GF, NB * T], F32R, o_act)
        act_lo = at("act_lo", [P, 2, GF, NB * T], F32R, o_act + 16384)
        k_hi = at("k_hi", [P, KVH, NB * T], F32R, o_act)
        k_lo = at("k_lo", [P, KVH, NB * T], F32R, o_act + 8192)
        v_hi = at("v_hi", [P, NB * T // P, KVH * HD], F32R, o_act + 16384)
        v_lo = at("v_lo", [P, NB * T // P, KVH * HD], F32R, o_act + 24576)
        hp = [at(f"hp{i}", [P, TP], F32, o_act + i * TP * 4) for i in range(4)]
        wsum = [at(f"wsum{i}", [P, TP], F32, o_act + (4 + i) * TP * 4) for i in range(2)]
        wsum_pool = [at(f"wsum_pool{i}", [P, TP], F32, o_act + (6 + i) * TP * 4) for i in range(4)]
        w_hi_t = at("w_hi_t", [P, RING, UNIT], F32R, o_ring)
        w_lo_t = at("w_lo_t", [P, RING, UNIT], F32R, o_ring + RING * UNIT * 4)
        raw = at("raw", [P, RAW, UNIT], F32, o_raw)
        xin = at("xin", [P, NB * T // P, D], F32, o_h)
        yout = at("yout", [P, NB * T // P, D], F32, o_h)
        tmp = [at(f"tmp{i}", [P, T], F32, o_tmp + i * T * 4) for i in range(8)]
        silu_t, full, sqr, stat = tmp[0:2], tmp[2:4], tmp[4:6], tmp[6:8]
        h_hi = {k: [half_hi[b if k < 3 else 1 - b] for b in range(NB)] for k in range(4)}
        h_lo = {k: [half_lo[b if k < 3 else 1 - b] for b in range(NB)] for k in range(4)}
        qg, rot, qsq, cos_t, sin_t = tmp[0:2], tmp[2:4], tmp[4:6], tmp[6], tmp[7]
        vec_in = at("vec_in", [N_VEC, P], F32, o_tmp)
        q_store = [[at(f"q_store{b}_{i}", [P, HEADS // 2, T], F32, o_ring + (i * RING + 2 + 2 * b) * UNIT * 4)
                    for i in range(2)] for b in range(NB)]
        prob = at("prob", [P, 4, T], F32, o_h)
        pt_hi = at("pt_hi", [P, 4, T], F32R, o_h + 8192)
        qs_hi = at("qs_hi", [P, 2, T], F32R, o_h + 16384)
        qs_lo = at("qs_lo", [P, 2, T], F32R, o_h + 20480)
        pt_lo = at("pt_lo", [P, 4, T], F32R, o_h + 24576)
        o_hi = [at("o_hi0", [P, HEADS, T], F32R, o_h + 32768), at("o_hi1", [P, HEADS, T], F32R, o_h)]
        o_lo = [at("o_lo0", [P, HEADS, T], F32R, o_h + 49152), at("o_lo1", [P, HEADS, T], F32R, o_h + 16384)]
        ident = at("ident", [P, P], F32, o_const)
        ones = at("ones", [P, P], F32, o_const + 512)
        vec = at("vec", [P, 64], F32, o_const + 1024)
        edge = at("edge", [P, len(WINDOWS), 2, EDGE], F32, o_const + 1280)
        nmax = at("nmax", [P, 8], F32, o_const + 1536)
        rsum = at("rsum", [P, 8], F32, o_const + 1568)
        rinv = at("rinv", [P, 8], F32, o_const + 1600)
        epst = at("epst", [P, 2], F32, o_const + 1632)
        q_inv = at("q_inv", [P, NB * HEADS * T // P], F32, o_const + 1664)
        raw_max = at("raw_max", [P, 8], F32, o_const + 1920)
        assert o_const + 1952 <= nc.sbuf_usable_end, (o_const, nc.sbuf_usable_end)

        bank = [ctx.enter_context(nc.psum_tensor(f"bank{i}", [P, T], F32)) for i in range(8)]
        b_gate, b_up, b_down = bank[0:2], bank[2:4], bank[4:8]
        b_score, b_out, b_turn, b_side = bank[0:2], bank[2], bank[3:6], bank[6:8]

        def sem(name):
            return ctx.enter_context(nc.semaphore(name))

        x_in = [sem(f"x_in{i}") for i in range(NB * T // P)]
        vec_landed, edge_landed = sem("vec_landed"), sem("edge_landed")
        ident_made, ones_made, pads_made, eps_made = sem("ident_made"), sem("ones_made"), sem("pads_made"), sem("eps_made")
        vec_turned, vec_ready = sem("vec_turned"), sem("vec_ready")
        x_turned, x_copied_act, x_copied_dve = sem("x_turned"), sem("x_copied_act"), sem("x_copied_dve")
        raw_in = [sem(f"raw_in{i}") for i in range(RAW)]
        w_hi, w_lo = sem("w_hi"), sem("w_lo")
        n_sq, n_acc, n_ms, n_sqrt = sem("n_sq"), sem("n_acc"), sem("n_ms"), sem("n_sqrt")
        n_rstd, n_full, n_hi, n_lo = sem("n_rstd"), sem("n_full"), sem("n_hi"), sem("n_lo")
        m_row, m_step, m_pstep, m_psum = sem("m_row"), sem("m_step"), sem("m_pstep"), sem("m_psum")
        m_full, m_hi, m_lo = sem("m_full"), sem("m_hi"), sem("m_lo")
        m_filled, m_scaled, m_x = sem("m_filled"), sem("m_scaled"), sem("m_x")
        gate_done, up_done, silu_done, prod_done = sem("gate_done"), sem("up_done"), sem("silu_done"), sem("prod_done")
        act_hi_done, act_lo_done = sem("act_hi_done"), sem("act_lo_done")
        down_filled, down_added = sem("down_filled"), sem("down_added")
        proj_done, p_sq, p_gain, p_ms, p_sqrt = sem("proj_done"), sem("p_sq"), sem("p_gain"), sem("p_ms"), sem("p_sqrt")
        rot_in = [sem("rot_in0"), sem("rot_in1")]
        p_r, p_cos, p_sin, p_sum, p_fin, p_hi, p_done = (sem("p_r"), sem("p_cos"), sem("p_sin"), sem("p_sum"),
                                                        sem("p_fin"), sem("p_hi"), sem("p_done"))
        v_half = sem("v_half")
        v_filled, v_hi_done, v_lo_done, tables_in = sem("v_filled"), sem("v_hi_done"), sem("v_lo_done"), sem("tables_in")
        a_qhi, a_q, s_filled, a_max, a_exp = sem("a_qhi"), sem("a_q"), sem("s_filled"), sem("a_max"), sem("a_exp")
        a_rawmax = sem("a_rawmax")
        a_rinv, a_prob, pt_filled, a_pthi, a_ptlo = sem("a_rinv"), sem("a_prob"), sem("pt_filled"), sem("a_pthi"), sem("a_ptlo")
        o_filled, o_copied = sem("o_filled"), sem("o_copied")
        o0_pool_hi, o0_pool = sem("o0_pool_hi"), sem("o0_pool")
        o0_hi, o0_split, o1_hi, o1_split = sem("o0_hi"), sem("o0_split"), sem("o1_hi"), sem("o1_split")
        wo_filled, wo_added = sem("wo_filled"), sem("wo_added")
        y_turned, y_act, y_dve, y_out = sem("y_turned"), sem("y_act"), sem("y_dve"), sem("y_out")

        block = ctx.enter_context(nc.Block())

        def tok(b):
            return slice(b * T, (b + 1) * T)

        def slot(u):
            if U_QKV <= u < U_WO:
                return (u - U_QKV) % 2
            if U_WO <= u < U_FFN1:
                return (u - U_WO) % RING_WO
            if u >= U_FFN1:
                return (u - U_FFN1) % RING
            return (u - U_FFN0) % RING

        def gu_unit(layer, g, c, up):
            return U_FFN[layer] + (0 if g == 0 else 4 + 6 * (g - 1)) + 2 * c + up

        def down_unit(layer, g, c):
            return U_FFN[layer] + (4 + 6 * g + 4 if g < NG - 1 else N_FFN - 2) + c

        def q_of(h, b):
            return q_store[b][h // 4][:, h % 4, :]

        gu_rows = [w_gu[l].rearrange("(k p) f -> p k f", p=P) for l in range(2)]
        qkv_rows = w_qkv[0].rearrange("(k p) e -> p k e", p=P)
        wo_rows = w_o[0].rearrange("(k p) e -> p k e", p=P)

        @block.sync
        def _(sp):
            def load_unit(u, src, shape, w_lo_before=None):
                if w_lo_before is not None:
                    sp.wait_ge(w_lo, w_lo_before)
                elif u >= RAW:
                    sp.wait_ge(w_lo, u - RAW + 1)
                dst = raw[:, u % RAW, :]
                if shape:
                    dst = dst.rearrange("p (k f) -> p k f", k=shape)
                sp.dma_start(dst, src).then_inc(raw_in[u % RAW], 16)

            def load_gu(layer, g, j=None, g0=None):
                for c in range(GF):
                    for up in range(2):
                        u = gu_unit(layer, g if j is None else g0, c, up)
                        if j is None:
                            col = up * DFF + (GF * g + c) * P
                            load_unit(u, gu_rows[layer][:, :, col:col + P], KC)
                        else:
                            col = j * (BODIES * GF * P) + up * DFF + (GF * g0 + c) * P
                            load_unit(u, gu_rows[layer][:, :, bass.ds(col, P)], KC,
                                      j * (6 * BODIES) + u - RAW + 1)

            def load_down(layer, g, j=None, g0=None):
                for c in range(GF):
                    u = down_unit(layer, g if j is None else g0, c)
                    if j is None:
                        r = (GF * g + c) * P
                        load_unit(u, w_down[layer][r:r + P, :], 0)
                    else:
                        r = j * (BODIES * GF * P) + (GF * g0 + c) * P
                        load_unit(u, w_down[layer][bass.ds(r, P), :], 0, j * (6 * BODIES) + u - RAW + 1)

            def load_ffn(layer, skip=0):
                load_gu(layer, 0)
                with sp.Fori(0, LOOPS) as j:
                    for g0 in range(1, 1 + BODIES):
                        load_gu(layer, None, j, g0)
                        load_down(layer, None, j, g0 - 1)
                for g in range(FIRST_PEELED, NG):
                    load_gu(layer, g)
                    load_down(layer, g - 1)
                load_down(layer, NG - 1)

            for row, src in ((V_MIX, norm_mix.rearrange("l (c p) -> (l c) p", p=P)),
                             (V_FFN, norm_ffn.rearrange("l (c p) -> (l c) p", p=P)),
                             (V_PB, pool_b.rearrange("l g (c p) -> (l g c) p", p=P)),
                             (V_PS, pool_scale.rearrange("l (c p) -> (l c) p", p=P)),
                             (V_QG, q_gain), (V_KG, k_gain)):
                sp.dma_start(vec_in[row:row + src.shape[0], :], src).then_inc(vec_landed, 16)
            for i in range(NB * T // P):
                src = (x_prompt, x_sample)[i // 4][0]
                r = (i % 4) * P
                sp.dma_start(xin[:, i, :], src[r:r + P, :]).then_inc(x_in[i], 16)
            sp.dma_start(edge[:, :, :, :], edge_tab).then_inc(edge_landed, 16)
            for i in range(2):
                sp.dma_start(raw[:, i, :].rearrange("p (g k e) -> p g k e", g=2, k=2),
                             pool_w[0, 2 * i:2 * i + 2].rearrange("g (k p) e -> p g k e", p=P)
                             ).then_inc(raw_in[i], 16)
            load_ffn(0)

            def load_qkv(b, i):
                u = U_QKV + N_QKV * b + i
                if i < 2:
                    load_unit(u, qkv_rows[:, :, (HEADS + i) * HD:(HEADS + i + 1) * HD], KC)
                elif i < 4:
                    k0 = (i - 2) * 4
                    load_unit(u, qkv_rows[:, k0:k0 + 4, (HEADS + KVH) * HD:], 4)
                else:
                    load_unit(u, qkv_rows[:, :, (i - 4) * HD:(i - 3) * HD], KC)

            def load_attention(i):
                if i < NB * N_QKV:
                    load_qkv(i // N_QKV, i % N_QKV)
                elif U_QKV + i < U_FFN1:
                    m = (i - NB * N_QKV) % KC
                    load_unit(U_QKV + i, wo_rows[:, :, m * P:(m + 1) * P], KC)

            def rotate(p):
                sp.wait_ge(p_gain, p + 1)
                for dst, src in ((0, 1), (1, 0), (2, 3), (3, 2)):
                    sp.dma_start(rot[p % 2][32 * dst:32 * dst + 32, :],
                                 qg[p % 2][32 * src:32 * src + 32, :]).then_inc(rot_in[p % 2], 16)

            for i in range(RAW):
                load_attention(i)
            for i in range(NB * N_QKV):
                load_attention(i + RAW)
                b, j = i // N_QKV, i % N_QKV
                if i == 2:
                    sp.wait_ge(n_lo, 2 * 16)
                    sp.dma_start(cos_t[:, :], rope_cos).then_inc(tables_in, 16)
                    sp.dma_start(sin_t[:, :], rope_sin).then_inc(tables_in, 16)
                    for p in range(KVH):
                        rotate(p)
                elif b == 1 and j < 2:
                    rotate(N_PROJ * b + j)
                elif j >= 4:
                    rotate(N_PROJ * b + j - 2)
            for i in range(NB * N_QKV + RAW, U_FFN1 - U_QKV):
                load_attention(i)
            load_ffn(1)

            for i in range(NB * T // P):
                sp.wait_ge(y_act, i + 1)
                sp.wait_ge(y_dve, i + 1)
                dst = (y_prompt, y_sample)[i // 4][0]
                r = (i % 4) * P
                sp.dma_start(dst[r:r + P, :], yout[:, i, :]).then_inc(y_out, 16)
            sp.wait_ge(y_out, 16 * (NB * T // P))

        SEQ_AB = [(c, b) for b in range(NB) for c in range(KC)]
        SEQ = {0: SEQ_AB, 1: SEQ_AB, 2: SEQ_AB, 3: SEQ_AB}
        GAIN = {0: V_MIX, 1: V_FFN, 2: V_MIX + KC, 3: V_FFN + KC}

        def acc_index(k, r):
            return 14 * k + sum(1 for c, _ in SEQ[k][:r + 1] if c > 0)

        def wait_unit_used(eng, i):
            b, j = i // N_QKV, i % N_QKV
            if i >= NB * N_QKV:
                eng.wait_ge(wo_filled, i - NB * N_QKV + 1)
            elif j == 2:
                eng.wait_ge(v_half, b + 1)
            elif j == 3:
                eng.wait_ge(v_filled, 2 * (b + 1))
            else:
                eng.wait_ge(proj_done, N_PROJ * b + (j if j < 2 else j - 2) + 1)

        def following(i):
            return U_QKV + i + (2 if U_QKV + i < U_WO else RING_WO)

        def unit_of(kind, n):
            if kind == "w":
                return NB * N_QKV + n
            j = n % N_PROJ
            return N_QKV * (n // N_PROJ) + (j if j < 2 else j + 2)

        def q_cols(p):
            a = HEADS * (p // N_PROJ) + p % N_PROJ - KVH
            return slice(T // P * a, T // P * (a + 1))

        @block.tensor
        def _(pe):
            def product(out, parts, first, last, done=None):
                n = len(parts)
                for i, (w, m) in enumerate(parts):
                    ins = pe.matmul(out, w, m, start=first and i == 0, stop=last and i == n - 1)
                if done is not None:
                    ins.then_inc(done, 1)

            def three(whi, wlo, mhi, mlo):
                return [(whi, mhi), (whi, mlo), (wlo, mhi)]

            def w_chunk(u, k):
                return w_hi_t[:, slot(u), k * P:(k + 1) * P], w_lo_t[:, slot(u), k * P:(k + 1) * P]

            def mean_square(k, b, out):
                r = max(i for i, (_, bb) in enumerate(SEQ[k]) if bb == b)
                pe.wait_ge(n_acc, acc_index(k, r))
                pe.matmul(out[:, :], ones[:, :], stat[b][:, :], start=True, stop=True).then_inc(n_ms, 1)

            pe.wait_ge(ident_made, 2)
            pe.wait_ge(vec_landed, 6 * 16)
            pe.transpose(bank[0][:, 0:N_VEC], vec_in[:, :], ident[0:N_VEC, 0:N_VEC]).then_inc(vec_turned, 1)
            for q in range(2 * NB * T // P):
                i, half = q // 2, q % 2
                if half == 0:
                    pe.wait_ge(x_in[i], 16)
                if q >= 4:
                    if q % 2 == 0:
                        pe.wait_ge(x_copied_act, q // 2 - 1)
                    else:
                        pe.wait_ge(x_copied_dve, q // 2 - 1)
                for c in range(4):
                    ins = pe.transpose(b_down[q % 4][:, c * P:(c + 1) * P],
                                       xin[:, i, (4 * half + c) * P:(4 * half + c + 1) * P], ident[:, :])
                ins.then_inc(x_turned, 1)
            pe.wait_ge(ones_made, 1)
            mean_square(0, 0, bank[1])
            mean_square(0, 1, bank[2])

            for b in range(NB):
                for g in range(4):
                    pe.wait_ge(w_lo, g // 2 + 1)
                    pe.wait_ge(m_lo, KC * b + 2 * g + 2)
                    for m in range(2):
                        q = KC * b + 2 * g + m
                        if q >= 4:
                            pe.wait_ge(m_scaled, q - 3)
                        elif q == 0:
                            pe.wait_ge(x_copied_act, 8)
                            pe.wait_ge(x_copied_dve, 8)
                        parts = []
                        for k in range(2):
                            lo = (g % 2) * 512 + k * 256 + m * P
                            s = slot(g // 2)
                            parts += three(w_hi_t[:, s, lo:lo + P], w_lo_t[:, s, lo:lo + P],
                                           h_hi[0][b][:, 2 * g + k, :], h_lo[0][b][:, 2 * g + k, :])
                        product(b_down[q % 4][:, :], parts, True, True, m_filled)

            def gate_up_half(layer, g, c, b, up, t, norm=None, n=None):
                u = gu_unit(layer, g, c, up)
                parts = []
                out = (b_up if up else b_gate)[t % 2]
                for k in range(KC):
                    whi, wlo = w_chunk(u, k)
                    hk = 2 * layer + 1
                    parts = three(whi, wlo, h_hi[hk][b][:, k, :], h_lo[hk][b][:, k, :])
                    if norm is not None:
                        pe.wait_ge(n_lo, (norm - 1) * 16 + KC * b + k + 1)
                    product(out[:, :], parts, k == 0, k == KC - 1,
                            None if k < KC - 1 else (up_done if up else gate_done))

            def tile(layer, g, t, j=None, norm=None, between=None):
                c, b = t % 2, t // 2
                n = N_TILE * layer + 4 * g + t
                step = 0 if j is None else j * (4 * BODIES)
                ustep = 0 if j is None else j * (6 * BODIES)
                if 4 * g + t >= 2:
                    pe.wait_ge(prod_done, step + n - 1)
                for up in range(2):
                    if b == 0:
                        pe.wait_ge(w_lo, ustep + gu_unit(layer, g, c, up) + 1)
                    gate_up_half(layer, g, c, b, up, t, norm if up == 0 and c == 0 else None)
                    if between is not None and up == 0:
                        between()

            def down_bank(layer, g, b, m, j=None):
                i = KC * b + m
                q = N_DOWN * layer + 16 * g + i
                step = 0 if j is None else j * (16 * BODIES)
                if 16 * g + i >= 4:
                    pe.wait_ge(down_added, step + q - 3)
                parts = []
                for c in range(GF):
                    whi, wlo = w_chunk(down_unit(layer, g, c), m)
                    parts += three(whi, wlo, act_hi[:, g % 2, c, tok(b)], act_lo[:, g % 2, c, tok(b)])
                product(b_down[i % 4][:, :], parts, True, True, down_filled)

            def down(layer, g, j=None):
                tstep = 0 if j is None else j * (4 * BODIES)
                ustep = 0 if j is None else j * (6 * BODIES)
                pe.wait_ge(w_lo, ustep + down_unit(layer, g, 1) + 1)
                pe.wait_ge(act_lo_done, tstep + N_TILE * layer + 4 * (g + 1))
                for b in range(NB):
                    for m in range(KC):
                        down_bank(layer, g, b, m, j)

            def swiglu(layer, norm, ms_b1):
                for t in range(4):
                    tile(layer, 0, t, norm=norm, between=ms_b1 if t == 0 else None)
                with pe.Fori(0, LOOPS) as j:
                    for g in range(1, 1 + BODIES):
                        for t in range(4):
                            tile(layer, g, t, j)
                        down(layer, g - 1, j)
                for g in range(FIRST_PEELED, NG):
                    for t in range(4):
                        tile(layer, g, t)
                    down(layer, g - 1)

            def down_last(layer, inside):
                g = NG - 1
                pe.wait_ge(w_lo, down_unit(layer, g, 1) + 1)
                pe.wait_ge(act_lo_done, N_TILE * (layer + 1))
                for b in range(NB):
                    for m in range(KC):
                        down_bank(layer, g, b, m)
                        if b == 1 and m == 2 and inside is not None:
                            inside()

            mean_square(1, 0, bank[3])
            swiglu(0, 1, lambda: mean_square(1, 1, b_down[0]))
            down_last(0, lambda: mean_square(2, 0, bank[1]))

            def project(p, out, bank_free, quarter=None):
                b, u = p // N_PROJ, U_QKV + unit_of("p", p)
                if quarter in (None, 0):
                    if bank_free > 0:
                        pe.wait_ge(p_gain, bank_free)
                    pe.wait_ge(w_lo, u + 1)
                for k in range(KC) if quarter is None else range(2 * quarter, 2 * quarter + 2):
                    whi, wlo = w_chunk(u, k)
                    if p == 0:
                        pe.wait_ge(n_lo, 16 + k + 1)
                    product(out[:, :], three(whi, wlo, h_hi[2][b][:, k, :], h_lo[2][b][:, k, :]),
                            k == 0, k == KC - 1, proj_done if k == KC - 1 else None)
                    if k == 1 and p > 0 and p not in (KVH, N_PLAIN):
                        if p < N_PLAIN:
                            head_square(p - 1, b_up[(p - 1) % 2], p - 2)
                        else:
                            head_square(p - 1, b_side[1], p - 1)

            def head_square(p, out, bank_free):
                pe.wait_ge(p_sq, p + 1)
                if bank_free > 0:
                    pe.wait_ge(p_sqrt, bank_free)
                if p % N_PROJ >= KVH:
                    for i in range(T // P):
                        ins = pe.matmul(out[:, i:i + 1], qsq[p % 2][:, i * P:(i + 1) * P], ones[:, 0:1],
                                        start=True, stop=True)
                    ins.then_inc(p_ms, 1)
                    return
                pe.matmul(out[:, :], ones[:, :], qsq[p % 2][:, :], start=True, stop=True).then_inc(p_ms, 1)

            def values(b, banks, quarter):
                half = quarter // 2
                u = U_QKV + N_QKV * b + 2 + half
                if quarter % 2 == 0:
                    pe.wait_ge(w_lo, u + 1)
                for t in range(2 * (quarter % 2), 2 * (quarter % 2) + 2):
                    parts = []
                    for k in range(4 * half, 4 * half + 4):
                        c0 = (k % 4) * 256
                        hh = h_hi[2][b][:, k, t * P:(t + 1) * P]
                        hl = h_lo[2][b][:, k, t * P:(t + 1) * P]
                        wh, wl = w_hi_t[:, slot(u), c0:c0 + 256], w_lo_t[:, slot(u), c0:c0 + 256]
                        parts += [(hh, wh), (hh, wl), (hl, wh)]
                    out = banks[t // 2][:, (t % 2) * 256:(t % 2) * 256 + 256]
                    for i, (w, m) in enumerate(parts):
                        ins = pe.matmul(out, w, m, start=half == 0 and t % 2 == 0 and i == 0,
                                        stop=half == 1 and i == len(parts) - 1, skip_group_check=True)
                    if half == 0 and t == 3:
                        ins.then_inc(v_half, 1)
                    if half == 1 and t % 2 == 1:
                        ins.then_inc(v_filled, 1)

            project(0, b_gate[0], 0)
            mean_square(2, 1, b_down[3])
            project(1, b_gate[1], 0)
            for quarter in range(4):
                values(0, b_down[0:2], quarter)
                if quarter == 1:
                    head_square(1, b_up[1], 0)
            for p in range(KVH, N_PLAIN):
                project(p, b_gate[p % 2], p - 1)

            def score(a, i):
                b, kv = a // 8, a % 8 // 4
                if i == 0:
                    pe.wait_ge(a_q, a + 1)
                s = 4 * a + i
                if s >= 2:
                    pe.wait_ge(a_exp, s - 1)
                c = slice(i * P, (i + 1) * P)
                product(b_score[s % 2][:, :],
                        three(qs_hi[:, a % 2, c], qs_lo[:, a % 2, c], k_hi[:, kv, tok(b)], k_lo[:, kv, tok(b)]),
                        True, True, s_filled)

            def turn_probs(a, tiles):
                pe.wait_ge(a_prob, 4 * a + 4)
                for sc in tiles:
                    r = 4 * a + sc
                    if r >= 3:
                        pe.wait_ge(a_ptlo, r - 2)
                    for i in range(4):
                        ins = pe.transpose(b_turn[r % 3][:, i * P:(i + 1) * P], prob[:, i, sc * P:(sc + 1) * P],
                                           ident[:, :])
                    ins.then_inc(pt_filled, 1)

            def attend(a):
                b, kv = a // 8, a % 8 // 4
                if a >= 1:
                    pe.wait_ge(o_copied, a)
                for sc in range(4):
                    pe.wait_ge(a_ptlo, 4 * a + sc + 1)
                    t, c = 4 * b + sc, slice(kv * HD, (kv + 1) * HD)
                    product(b_out[:, :], three(v_hi[:, t, c], v_lo[:, t, c], pt_hi[:, sc, :], pt_lo[:, sc, :]),
                            sc == 0, sc == 3, o_filled if sc == 3 else None)

            def project_out(w, quarter=None):
                b, u = w // KC, U_WO + w
                if quarter in (None, 0):
                    pe.wait_ge(w_lo, u + 1)
                    if w >= 2:
                        pe.wait_ge(wo_added, w - 1)
                    else:
                        pe.wait_ge(p_sqrt, NB * N_PROJ)
                for k in range(HEADS) if quarter is None else range(2 * quarter, 2 * quarter + 2):
                    if w == KC:
                        pe.wait_ge(o1_split, k + 1)
                    elif w == 0:
                        pe.wait_ge(o0_pool if k < 6 else o0_split, k % 6 + 1)
                    whi, wlo = w_chunk(u, k)
                    product(b_side[w % 2][:, :], three(whi, wlo, o_hi[b][:, k, :], o_lo[b][:, k, :]),
                            k == 0, k == HEADS - 1, wo_filled if k == HEADS - 1 else None)

            def beside(a, i):
                kind, n = BESIDE[a]
                if kind == "p":
                    if a == 0 and i == 0:
                        pe.wait_ge(v_lo_done, 4)
                    project(n, b_side[0], n, i)
                elif kind == "v":
                    values(1, b_side, i)
                elif kind == "w":
                    project_out(n, i)
                elif i == 0:
                    head_square(n, b_side[1], n)

            beside(-1, 0)
            head_square(N_PLAIN - 1, b_up[1], N_PLAIN - 2)
            beside(-1, 1)
            pe.wait_ge(p_gain, N_PLAIN)
            for i in range(4):
                score(0, i)
                if i in (1, 2):
                    beside(-1, i + 1)
            pe.wait_ge(p_sqrt, N_PLAIN)
            pe.wait_ge(v_lo_done, 2)
            for a in range(16):
                turn_probs(a, range(3))
                for i in range(4):
                    beside(a, i)
                    if a + 1 < 16:
                        score(a + 1, i)
                    if i == 0:
                        turn_probs(a, [3])
                attend(a)

            for w in range(7, 16):
                project_out(w)
                if w == 9:
                    mean_square(3, 0, bank[1])
            swiglu(1, 3, lambda: mean_square(3, 1, b_down[0]))
            down_last(1, None)

            for q in range(2 * NB * T // P):
                i, half = q // 2, q % 2
                if q % 8 == 0:
                    pe.wait_ge(down_added, N_DOWN * 2 - 8 + q)
                if q >= 4:
                    if half == 0:
                        pe.wait_ge(y_act, q // 2 - 1)
                    else:
                        pe.wait_ge(y_dve, q // 2 - 1)
                for c in range(4):
                    ins = pe.transpose(bank[q % 4][:, c * P:(c + 1) * P],
                                       x[:, 4 * half + c, i * P:(i + 1) * P], ident[:, :])
                ins.then_inc(y_turned, 1)

        @block.scalar
        def _(act):
            def split_hi(u, step=None):
                if step is None:
                    act.wait_ge(raw_in[u % RAW], 16 * (u // RAW + 1))
                else:
                    act.wait_ge(raw_in[u % RAW], step * (16 * 6 * BODIES // RAW) + 16 * (u // RAW + 1))
                nc.scalar.copy(w_hi_t[:, slot(u), :], raw[:, u % RAW, :]).then_inc(w_hi, 1)

            def square(k, r, ready):
                c, b = SEQ[k][r]
                ready(c, b)
                if c == 0:
                    dst = stat[b]
                else:
                    i = acc_index(k, r)
                    if i % 14 != 1 and i > 2 or k > 0:
                        act.wait_ge(n_acc, i - 2)
                    dst = sqr[i % 2]
                nc.scalar.activation(dst[:, :], x[:, c, tok(b)], ACT.Square).then_inc(n_sq, 1)

            def root(k, b, src):
                act.wait_ge(n_ms, 2 * k + b + 1)
                nc.scalar.activation(stat[b][:, :], src[:, :], ACT.Sqrt, bias=epst[:, 0:1],
                                     scale=1.0 / D).then_inc(n_sqrt, 1)

            def norm_hi(k, b, c):
                i = 16 * (k - 1) + KC * b + c
                act.wait_ge(n_full, i + 1)
                nc.scalar.copy(h_hi[k][b][:, c, :], full[i % 2][:, :]).then_inc(n_hi, 1)

            for i in range(NB * T // P):
                act.wait_ge(x_turned, 2 * i + 1)
                nc.scalar.copy(x[:, 0:4, i * P:(i + 1) * P],
                               b_down[(2 * i) % 4][:, :].rearrange("p (c t) -> p c t", c=4)).then_inc(x_copied_act, 1)
            act.wait_ge(x_turned, 16)

            def x_here(c, b):
                act.wait_ge(x_copied_act, 4 * (b + 1))
                act.wait_ge(x_copied_dve, 4 * (b + 1))

            act.wait_ge(eps_made, 2)
            for r in range(8):
                square(0, r, x_here)
            root(0, 0, bank[1])
            split_hi(0)
            split_hi(1)
            for r in range(8, 16):
                square(0, r, x_here)
            root(0, 1, bank[2])

            def scaled(q):
                c = q % KC
                act.wait_ge(m_filled, q + 1)
                if q >= 2:
                    act.wait_ge(m_x, q - 1)
                else:
                    act.wait_ge(vec_ready, 2)
                nc.scalar.activation(silu_t[q % 2][:, :], b_down[q % 4][:, :], ACT.Identity,
                                     bias=vec[:, V_BS + c:V_BS + c + 1],
                                     scale=vec[:, V_PS + c:V_PS + c + 1]).then_inc(m_scaled, 1)

            def x_mixed(c, b):
                act.wait_ge(m_x, KC * b + c + 1)
                if c == 0:
                    act.wait_ge(m_row, KC * (b + 1))

            for i in range(16):
                b, c = i // KC, i % KC
                act.wait_ge(m_full, i + 1)
                nc.scalar.copy(h_hi[0][b][:, c, :], full[i % 2][:, :]).then_inc(m_hi, 1)
                if 4 <= i < 14 and i % 2 == 1:
                    scaled(i - 5)
                    scaled(i - 4)
            for r in range(8):
                square(1, r, x_mixed)
            for q in range(10, 16):
                scaled(q)
            for i in range(4):
                split_hi(U_FFN0 + i)
            act.wait_ge(m_filled, 16)
            root(1, 0, bank[3])
            for c in range(KC):
                square(1, 8 + c, x_mixed)
                norm_hi(1, 0, c)
            for i in range(4, 6):
                split_hi(U_FFN0 + i)
            root(1, 1, b_down[0])
            for c in range(KC):
                norm_hi(1, 1, c)

            def silu(layer, g, t, j=None):
                i = 4 * g + t
                n = N_TILE * layer + i
                step = 0 if j is None else j * (4 * BODIES)
                act.wait_ge(gate_done, step + n + 1)
                if i >= 2:
                    act.wait_ge(prod_done, step + n - 1)
                nc.scalar.activation(silu_t[t % 2][:, :], b_gate[t % 2][:, :], ACT.Silu).then_inc(silu_done, 1)

            def hidden_hi(layer, g, t, j=None):
                c, b = t % 2, t // 2
                step = 0 if j is None else j * (4 * BODIES)
                act.wait_ge(prod_done, step + N_TILE * layer + 4 * g + t + 1)
                nc.scalar.copy(act_hi[:, g % 2, c, tok(b)], full[t % 2][:, :]).then_inc(act_hi_done, 1)

            def group(layer, g, j=None):
                tstep = 0 if j is None else j * (4 * BODIES)
                dstep = 0 if j is None else j * (16 * BODIES)
                for t in range(4):
                    silu(layer, g, t, j)
                    hidden_hi(layer, g, t, j)
                    if t >= 2:
                        act.wait_ge(up_done, tstep + N_TILE * layer + 4 * g + t + 1)
                        for up in range(2):
                            u = gu_unit(layer, g, t - 2, up) + RING
                            if u < U_FFN[layer] + N_FFN or (layer == 0 and slot(u) < 2):
                                split_hi(u, j)
                if g >= 1 and down_unit(layer, g - 1, 0) + RING < U_FFN[layer] + N_FFN:
                    act.wait_ge(down_filled, dstep + N_DOWN * layer + 16 * g)
                    for c in range(GF):
                        split_hi(down_unit(layer, g - 1, c) + RING, j)

            def swiglu(layer):
                group(layer, 0)
                with act.Fori(0, LOOPS) as j:
                    for g in range(1, 1 + BODIES):
                        group(layer, g, j)
                for g in range(FIRST_PEELED, NG):
                    group(layer, g)

            swiglu(0)

            def x_ffn0(c, b):
                act.wait_ge(down_added, N_DOWN - 16 + KC * b + c + 1)

            for r in range(8):
                square(2, r, x_ffn0)
            root(2, 0, bank[1])
            for c in range(KC):
                square(2, 8 + c, x_ffn0)
                norm_hi(2, 0, c)

            def gain(p, src):
                act.wait_ge(proj_done, p + 1)
                if p >= 2:
                    act.wait_ge(p_done, p - 1)
                    act.wait_ge(p_ms, p - 1)
                else:
                    act.wait_ge(n_acc, 3 * 14)
                g = V_KG if p % N_PROJ < KVH else V_QG
                nc.scalar.activation(qsq[p % 2][:, :], src[:, :], ACT.Square).then_inc(p_sq, 1)
                nc.scalar.activation(qg[p % 2][:, :], src[:, :], ACT.Copy,
                                     scale=vec[:, g:g + 1]).then_inc(p_gain, 1)

            def head_root(p, src):
                act.wait_ge(p_ms, p + 1)
                if p % N_PROJ < KVH:
                    nc.scalar.activation(qsq[p % 2][:, :], src[:, :], ACT.Sqrt, bias=epst[:, 0:1],
                                         scale=1.0 / HD).then_inc(p_sqrt, 1)
                else:
                    nc.scalar.activation(q_inv[:, q_cols(p)], src[:, 0:T // P], ACT.Sqrt,
                                         bias=epst[:, 1:2]).then_inc(p_sqrt, 1)

            def key_hi(p):
                b, j = p // N_PROJ, p % N_PROJ
                act.wait_ge(p_fin, KVH * b + j + 1)
                nc.scalar.copy(k_hi[:, j, tok(b)], rot[p % 2][:, :]).then_inc(p_hi, 1)

            def split_next(i):
                wait_unit_used(act, i)
                split_hi(following(i))

            def values_hi(b, banks):
                for t in range(2):
                    act.wait_ge(v_filled, 2 * b + t + 1)
                    nc.scalar.copy(v_hi[:, 4 * b + 2 * t:4 * b + 2 * t + 2, :],
                                   banks[t][:, :].rearrange("p (t f) -> p t f", t=2)).then_inc(v_hi_done, 1)

            gain(0, b_gate[0])
            split_next(0)
            root(2, 1, b_down[3])
            for c in range(4):
                norm_hi(2, 1, c)
            gain(1, b_gate[1])
            split_next(1)
            for c in range(4, KC):
                norm_hi(2, 1, c)
            split_next(2)
            head_root(0, b_up[0])
            head_root(1, b_up[1])
            split_next(3)
            key_hi(0)
            gain(2, b_gate[0])
            key_hi(1)
            values_hi(0, b_down)
            split_next(4)
            for p in range(3, N_PLAIN):
                gain(p, b_gate[p % 2])
                split_next(unit_of("p", p))
                head_root(p - 1, b_up[(p - 1) % 2])

            def exps(a, tiles=range(4)):
                for i in tiles:
                    s = 4 * a + i
                    act.wait_ge(a_max, s + 1)
                    if a >= 1:
                        act.wait_ge(pt_filled, 4 * a)
                    else:
                        act.wait_ge(proj_done, N_PROJ)
                    nc.scalar.activation(prob[:, i, :], b_score[s % 2][:, :], ACT.Exp, bias=nmax[:, s % 8:s % 8 + 1], scale=q_inv[:, s:s + 1],
                                         accum_out=rsum[:, s % 8:s % 8 + 1]).then_inc(a_exp, 1)

            def x_attn(c, b):
                act.wait_ge(wo_added, KC * b + c + 1)
                if c == 0 and b == 0:
                    act.wait_ge(p_cos, NB * N_PROJ)
                    act.wait_ge(p_done, NB * N_PROJ)

            head_root(N_PLAIN - 1, b_up[1])
            key_hi(N_PROJ)
            exps(0)
            split_next(N_QKV + 2)
            values_hi(1, b_side)
            split_next(N_QKV + 3)
            key_hi(N_PROJ + 1)
            for a in range(16):
                kind, n = BESIDE[a]
                for sc in range(4):
                    r = 4 * a + sc
                    act.wait_ge(pt_filled, r + 1)
                    if a >= 1:
                        act.wait_ge(o_filled, a)
                    nc.scalar.copy(pt_hi[:, sc, :], b_turn[r % 3][:, :]).then_inc(a_pthi, 1)
                if a + 1 < 16:
                    exps(a + 1)
                else:
                    for h in range(4):
                        act.wait_ge(o_copied, 8 + h + 1)
                        nc.scalar.copy(o_hi[1][:, h, :], q_of(h, 1)).then_inc(o1_hi, 1)
                if kind == "p":
                    gain(n, b_side[0])
                    if n > N_PLAIN:
                        head_root(n - 1, b_side[1])
                    split_next(unit_of("p", n))
                elif kind == "s":
                    head_root(n, b_side[1])
                    for h in range(6, HEADS):
                        act.wait_ge(proj_done, NB * N_PROJ)
                        act.wait_ge(o_copied, h + 1)
                        nc.scalar.copy(o_hi[0][:, h, :], q_of(h, 0)).then_inc(o0_hi, 1)
                else:
                    if n >= 1:
                        square(3, n - 1, x_attn)
                    if a == 9:
                        act.wait_ge(o0_pool, 6)
                        act.wait_ge(o0_split, 2)
                        split_hi(U_WO + 2)
                        split_hi(U_WO + 3)
                    split_next(unit_of("w", n))
                act.wait_ge(o_filled, a + 1)
                nc.scalar.copy(q_of(a % 8, a // 8), b_out[:, :]).then_inc(o_copied, 1)
            for h in range(4, HEADS):
                act.wait_ge(o_copied, 8 + h + 1)
                nc.scalar.copy(o_hi[1][:, h, :], q_of(h, 1)).then_inc(o1_hi, 1)
            square(3, 6, x_attn)

            split_next(unit_of("w", 7))
            square(3, 7, x_attn)
            split_next(unit_of("w", 8))
            root(3, 0, bank[1])
            for c in range(KC):
                norm_hi(3, 0, c)
                square(3, 8 + c, x_attn)
                if c < KC - 1:
                    split_next(unit_of("w", 9 + c))
            act.wait_ge(o1_split, HEADS)
            for i in range(RING_WO, RING):
                split_hi(U_FFN1 + i)
            root(3, 1, b_down[0])
            for c in range(KC):
                norm_hi(3, 1, c)
            swiglu(1)

            for i in range(NB * T // P):
                act.wait_ge(y_turned, 2 * i + 1)
                nc.scalar.copy(yout[:, i, 0:512], bank[(2 * i) % 4][:, :]).then_inc(y_act, 1)

        @block.vector
        def _(dve):
            def split_lo(u, step=None):
                dve.wait_ge(w_hi, u + 1 if step is None else step * (6 * BODIES) + u + 1)
                nc.vector.tensor_tensor(w_lo_t[:, slot(u), :], raw[:, u % RAW, :],
                                        w_hi_t[:, slot(u), :].bitcast(F32), ALU.subtract).then_inc(w_lo, 1)

            def inverse(k, b):
                dve.wait_ge(n_sqrt, 2 * k + b + 1)
                nc.vector.reciprocal(stat[b][:, :], stat[b][:, :]).then_inc(n_rstd, 1)

            def norm_full(k, b, c):
                i = 16 * (k - 1) + KC * b + c
                dve.wait_ge(n_rstd, 2 * k + b + 1)
                if i >= 2:
                    dve.wait_ge(n_lo, i - 1)
                g = GAIN[k] + c
                nc.vector.scalar_tensor_tensor(full[i % 2][:, :], x[:, c, tok(b)], vec[:, g:g + 1], stat[b][:, :],
                                               ALU.mult, ALU.mult).then_inc(n_full, 1)

            def norm_lo(k, b, c):
                i = 16 * (k - 1) + KC * b + c
                dve.wait_ge(n_hi, i + 1)
                nc.vector.tensor_tensor(h_lo[k][b][:, c, :], full[i % 2][:, :], h_hi[k][b][:, c, :].bitcast(F32),
                                        ALU.subtract).then_inc(n_lo, 1)

            def norm_batch(k, b, before=None):
                for c in range(4 if before is not None else 0):
                    before(c)
                inverse(k, b)
                for c in range(KC):
                    if before is not None and c + 4 < KC:
                        before(c + 4)
                    norm_full(k, b, c)
                    if c >= 1:
                        norm_lo(k, b, c - 1)
                norm_lo(k, b, KC - 1)

            dve.wait_ge(vec_turned, 1)
            nc.vector.tensor_copy(vec[:, 0:N_VEC], bank[0][:, 0:N_VEC]).then_inc(vec_ready, 1)
            dve.wait_ge(vec_ready, 1)
            nc.vector.tensor_tensor(vec[:, V_BS:V_BS + KC], vec[:, V_PB:V_PB + KC], vec[:, V_PS:V_PS + KC],
                                    ALU.mult).then_inc(vec_ready, 1)
            for i in range(NB * T // P):
                dve.wait_ge(x_turned, 2 * i + 2)
                nc.vector.tensor_copy(x[:, 4:8, i * P:(i + 1) * P],
                                      b_down[(2 * i + 1) % 4][:, :].rearrange("p (c t) -> p c t", c=4)
                                      ).then_inc(x_copied_dve, 1)

            steps = [0]

            def chain(ins):
                steps[0] += 1
                ins.then_inc(m_step, 1)
                dve.wait_ge(m_step, steps[0])

            def row(b, c):
                i = KC * b + c
                if i >= 4:
                    dve.wait_ge(m_full, i - 3)
                nc.vector.scalar_tensor_tensor(hp[i % 4][:, PAD:PAD + T], x[:, c, tok(b)],
                                               vec[:, V_MIX + c:V_MIX + c + 1], stat[b][:, :],
                                               ALU.mult, ALU.mult).then_inc(m_row, 1)

            def pooled(b, c, win):
                i = KC * b + c
                ends = win[:, PAD:PAD + T].rearrange("p (n e) -> p n e", e=EDGE)[:, 0:T // EDGE:T // EDGE - 1, :]
                chain(nc.vector.tensor_tensor(ends, ends, edge[:, c // 2, :, :], ALU.mult))
                if i >= 2:
                    dve.wait_ge(m_lo, i - 1)
                nc.vector.scalar_tensor_tensor(full[i % 2][:, :], win[:, PAD:PAD + T], 1.0 / WINDOWS[c // 2],
                                               hp[i % 4][:, PAD:PAD + T], ALU.mult, ALU.subtract
                                               ).then_inc(m_full, 1)

            def pooled_lo(b, c):
                i = KC * b + c
                dve.wait_ge(m_hi, i + 1)
                nc.vector.tensor_tensor(h_lo[0][b][:, c, :], full[i % 2][:, :], h_hi[0][b][:, c, :].bitcast(F32),
                                        ALU.subtract).then_inc(m_lo, 1)

            dve.wait_ge(pads_made, 4)
            dve.wait_ge(edge_landed, 16)
            for b in range(NB):
                inverse(0, b)
                dve.wait_ge(n_rstd, b + 1)
                if b == 0:
                    split_lo(0)
                    split_lo(1)
                for pair in range(4):
                    even, odd = 2 * pair, 2 * pair + 1
                    row(b, odd)
                    row(b, even)
                    dve.wait_ge(m_row, KC * b + 2 * pair + 2)
                    if pair >= 1:
                        dve.wait_ge(m_psum, 4 * b + pair)
                        pooled(b, odd - 2, wsum_pool[2 * (pair - 1) % 4 + (pair - 1) % 2])
                        pooled_lo(b, odd - 2)
                    elif b >= 1:
                        dve.wait_ge(m_lo, KC)
                    win = window_sums(nc.vector, hp[(KC * b + even) % 4], wsum, pair + 1, chain)
                    pooled(b, even, win)
                    pooled_lo(b, even)
                dve.wait_ge(m_psum, 4 * b + 4)
                pooled(b, KC - 1, wsum_pool[2 * 3 % 4 + 3 % 2])
                pooled_lo(b, KC - 1)

            for i in range(4):
                split_lo(U_FFN0 + i)
            norm_batch(1, 0)
            for i in range(4, 6):
                split_lo(U_FFN0 + i)
            norm_batch(1, 1)

            def hidden(layer, g, t, j=None):
                c, b = t % 2, t // 2
                i = 4 * g + t
                n = N_TILE * layer + i
                step = 0 if j is None else j * (4 * BODIES)
                dve.wait_ge(silu_done, step + n + 1)
                dve.wait_ge(up_done, step + n + 1)
                if i >= 2:
                    dve.wait_ge(act_lo_done, step + n - 1)
                else:
                    dve.wait_ge(n_lo, 16 if layer == 0 else 48)
                nc.vector.tensor_tensor(full[t % 2][:, :], silu_t[t % 2][:, :], b_up[t % 2][:, :],
                                        ALU.mult).then_inc(prod_done, 1)
                dve.wait_ge(act_hi_done, step + n + 1)
                nc.vector.tensor_tensor(act_lo[:, g % 2, c, tok(b)], full[t % 2][:, :],
                                        act_hi[:, g % 2, c, tok(b)].bitcast(F32), ALU.subtract
                                        ).then_inc(act_lo_done, 1)

            def add_down(layer, g, i, j=None):
                q = N_DOWN * layer + 16 * g + i
                step = 0 if j is None else j * (16 * BODIES)
                dve.wait_ge(down_filled, step + q + 1)
                xc = x[:, i % KC, tok(i // KC)]
                nc.vector.tensor_tensor(xc, b_down[i % 4][:, :], xc, ALU.add).then_inc(down_added, 1)

            def group(layer, g, j=None):
                for t in range(4):
                    hidden(layer, g, t, j)
                    if t >= 2:
                        for up in range(2):
                            u = gu_unit(layer, g, t - 2, up) + RING
                            if u < U_FFN[layer] + N_FFN or (layer == 0 and slot(u) < 2):
                                split_lo(u, j)
                if g >= 1:
                    for i in range(16):
                        add_down(layer, g - 1, i, j)
                    if down_unit(layer, g - 1, 0) + RING < U_FFN[layer] + N_FFN:
                        for c in range(GF):
                            split_lo(down_unit(layer, g - 1, c) + RING, j)

            def swiglu(layer):
                group(layer, 0)
                with dve.Fori(0, LOOPS) as j:
                    for g in range(1, 1 + BODIES):
                        group(layer, g, j)
                for g in range(FIRST_PEELED, NG):
                    group(layer, g)

            swiglu(0)
            for i in range(KC):
                add_down(0, NG - 1, i)
            norm_batch(2, 0, before=lambda c: add_down(0, NG - 1, KC + c))

            def head_inverse(p):
                inv = qsq[p % 2][:, :] if p % N_PROJ < KVH else q_inv[:, q_cols(p)]
                dve.wait_ge(p_sqrt, p + 1)
                nc.vector.reciprocal(inv, inv).then_inc(p_r, 1)

            def rope(p):
                s, b, j = p % 2, p // N_PROJ, p % N_PROJ
                dve.wait_ge(rot_in[s], 64 * (p // 2 + 1))
                dve.wait_ge(tables_in, 32)
                nc.vector.tensor_tensor(rot[s][:, :], rot[s][:, :], sin_t[:, :], ALU.mult).then_inc(p_sin, 1)
                dve.wait_ge(p_cos, p + 1)
                dve.wait_ge(p_sin, p + 1)
                if j < KVH:
                    nc.vector.tensor_tensor(qg[s][:, :], qg[s][:, :], rot[s][:, :], ALU.add).then_inc(p_sum, 1)
                    dve.wait_ge(p_sum, KVH * b + j + 1)
                    dve.wait_ge(p_r, p + 1)
                    nc.vector.tensor_tensor(rot[s][:, :], qg[s][:, :], qsq[s][:, :], ALU.mult).then_inc(p_fin, 1)
                else:
                    nc.vector.tensor_tensor(q_of(j - KVH, b), qg[s][:, :], rot[s][:, :], ALU.add).then_inc(p_done, 1)

            def key_lo(p):
                s, b, j = p % 2, p // N_PROJ, p % N_PROJ
                dve.wait_ge(p_hi, KVH * b + j + 1)
                nc.vector.tensor_tensor(k_lo[:, j, tok(b)], rot[s][:, :], k_hi[:, j, tok(b)].bitcast(F32),
                                        ALU.subtract).then_inc(p_done, 1)

            def split_next(i):
                split_lo(following(i))

            def values_lo(b, banks):
                for t in range(2):
                    dve.wait_ge(v_hi_done, 2 * b + t + 1)
                    tt = slice(4 * b + 2 * t, 4 * b + 2 * t + 2)
                    nc.vector.tensor_tensor(v_lo[:, tt, :], banks[t][:, :].rearrange("p (t f) -> p t f", t=2),
                                            v_hi[:, tt, :].bitcast(F32), ALU.subtract).then_inc(v_lo_done, 1)

            split_next(0)
            inverse(2, 1)
            for c in range(5):
                norm_full(2, 1, c)
                if c >= 1:
                    norm_lo(2, 1, c - 1)
            split_next(1)
            for c in range(5, KC):
                norm_full(2, 1, c)
                norm_lo(2, 1, c - 1)
            norm_lo(2, 1, KC - 1)
            split_next(2)
            head_inverse(0)
            split_next(3)
            rope(0)
            key_lo(0)
            head_inverse(1)
            rope(1)
            key_lo(1)
            values_lo(0, b_down)
            split_next(4)
            for p in range(3, N_PLAIN):
                head_inverse(p - 1)
                if p < N_PLAIN - 1:
                    rope(p - 1)
                split_next(unit_of("p", p))

            def row_max(s):
                dve.wait_ge(s_filled, s + 1)
                if s >= 8:
                    dve.wait_ge(a_prob, s - 7)
                col = slice(s % 8, s % 8 + 1)
                nc.vector.tensor_reduce(raw_max[:, col], b_score[s % 2][:, :], AX.X, ALU.max,
                                        negate=True).then_inc(a_rawmax, 1)
                dve.wait_ge(a_rawmax, s + 1)
                if s % (T // P) == 0:
                    a = s // (T // P)
                    dve.wait_ge(p_r, N_PROJ * (a // HEADS) + KVH + a % HEADS + 1)
                nc.vector.tensor_tensor(nmax[:, col], raw_max[:, col], q_inv[:, s:s + 1], ALU.mult).then_inc(a_max, 1)

            def normalise(s):
                dve.wait_ge(a_exp, s + 1)
                col = slice(s % 8, s % 8 + 1)
                nc.vector.reciprocal(rinv[:, col], rsum[:, col]).then_inc(a_rinv, 1)
                dve.wait_ge(a_rinv, s + 1)
                nc.vector.tensor_scalar(prob[:, s % 4, :], prob[:, s % 4, :], rinv[:, col], None,
                                        ALU.mult).then_inc(a_prob, 1)

            def softmax(a, part):
                for i in range(2 * part, 2 * part + 2):
                    row_max(4 * a + i)
                    if i > 0:
                        normalise(4 * a + i - 1)
                if part == 1:
                    normalise(4 * a + 3)

            def add_wo(w):
                dve.wait_ge(wo_filled, w + 1)
                xc = x[:, w % KC, tok(w // KC)]
                nc.vector.tensor_tensor(xc, b_side[w % 2][:, :], xc, ALU.add).then_inc(wo_added, 1)

            rope(N_PROJ)
            key_lo(N_PROJ)
            head_inverse(N_PROJ + 1)
            softmax(0, 0)
            rope(N_PROJ + 1)
            softmax(0, 1)
            split_next(N_QKV + 2)
            values_lo(1, b_side)
            split_next(N_QKV + 3)
            key_lo(N_PROJ + 1)
            for a in range(16):
                kind, n = BESIDE[a]
                for sc in range(4):
                    r = 4 * a + sc
                    dve.wait_ge(a_pthi, r + 1)
                    nc.vector.tensor_tensor(pt_lo[:, sc, :], b_turn[r % 3][:, :], pt_hi[:, sc, :].bitcast(F32),
                                            ALU.subtract).then_inc(a_ptlo, 1)
                if a + 1 < 16:
                    softmax(a + 1, 0)
                if kind == "p" and n > N_PLAIN:
                    rope(n - 1)
                elif kind == "s":
                    rope(n)
                if a + 1 < 16:
                    softmax(a + 1, 1)
                else:
                    for h in range(4):
                        dve.wait_ge(o1_hi, h + 1)
                        nc.vector.tensor_tensor(o_lo[1][:, h, :], q_of(h, 1), o_hi[1][:, h, :].bitcast(F32),
                                                ALU.subtract).then_inc(o1_split, 1)
                if kind == "p":
                    if n > N_PLAIN:
                        head_inverse(n - 1)
                    split_next(unit_of("p", n))
                elif kind == "s":
                    head_inverse(n)
                    for h in range(6, HEADS):
                        dve.wait_ge(o0_hi, h - 5)
                        nc.vector.tensor_tensor(o_lo[0][:, h, :], q_of(h, 0), o_hi[0][:, h, :].bitcast(F32),
                                                ALU.subtract).then_inc(o0_split, 1)
                else:
                    add_wo(n)
                    if a == 9:
                        split_lo(U_WO + 2)
                        split_lo(U_WO + 3)
                    split_next(unit_of("w", n))
            for h in range(4, HEADS):
                dve.wait_ge(o1_hi, h + 1)
                nc.vector.tensor_tensor(o_lo[1][:, h, :], q_of(h, 1), o_hi[1][:, h, :].bitcast(F32),
                                        ALU.subtract).then_inc(o1_split, 1)

            add_wo(7)
            split_next(unit_of("w", 7))
            add_wo(8)
            split_next(unit_of("w", 8))
            inverse(3, 0)
            norm_full(3, 0, 0)
            for c in range(1, KC):
                norm_full(3, 0, c)
                norm_lo(3, 0, c - 1)
                add_wo(8 + c)
                split_next(unit_of("w", 8 + c))
            norm_lo(3, 0, KC - 1)
            for i in range(RING_WO, RING):
                split_lo(U_FFN1 + i)
            norm_batch(3, 1)
            swiglu(1)
            for i in range(16):
                add_down(1, NG - 1, i)

            for i in range(NB * T // P):
                dve.wait_ge(y_turned, 2 * i + 2)
                nc.vector.tensor_copy(yout[:, i, 512:1024], bank[(2 * i + 1) % 4][:, :]).then_inc(y_dve, 1)

        @block.gpsimd
        def _(pool):
            nc.gpsimd.memset(ident[:, :], 0.0).then_inc(ident_made, 1)
            pool.wait_ge(ident_made, 1)
            nc.gpsimd.affine_select(out=ident[:, :], in_=ident[:, :], compare_op=ALU.not_equal, fill=1.0,
                                    base=0, pattern=[[-1, P]], channel_multiplier=1).then_inc(ident_made, 1)
            nc.gpsimd.memset(ones[:, :], 1.0).then_inc(ones_made, 1)
            nc.gpsimd.memset(epst[:, 0:1], EPS).then_inc(eps_made, 1)
            nc.gpsimd.memset(epst[:, 1:2], EPS * HD).then_inc(eps_made, 1)
            for i in range(4):
                nc.gpsimd.memset(hp[i][:, :], 0.0).then_inc(pads_made, 1)

            def add_squares(k, r):
                c, b = SEQ[k][r]
                if c == 0:
                    return
                i = acc_index(k, r)
                pool.wait_ge(n_sq, 16 * k + r + 1)
                if i >= 2:
                    pool.wait_ge(n_acc, i - 1)
                nc.gpsimd.tensor_tensor(out=stat[b][:, :], in0=stat[b][:, :], in1=sqr[i % 2][:, :],
                                        op=ALU.add).then_inc(n_acc, 1)

            for r in range(16):
                add_squares(0, r)

            steps = [0]

            def chain(ins):
                steps[0] += 1
                ins.then_inc(m_pstep, 1)
                pool.wait_ge(m_pstep, steps[0])

            def add_mixed(q):
                b, c = q // KC, q % KC
                pool.wait_ge(m_scaled, q + 1)
                nc.gpsimd.tensor_tensor(out=x[:, c, tok(b)], in0=x[:, c, tok(b)], in1=silu_t[q % 2][:, :],
                                        op=ALU.add).then_inc(m_x, 1)

            for b in range(NB):
                for pair in range(4):
                    i = 4 * b + pair
                    pool.wait_ge(m_row, 2 * i + 1)
                    if i >= 2:
                        pool.wait_ge(m_full, 2 * (i - 2) + 2)
                    bufs = wsum_pool[2 * (pair % 2):2 * (pair % 2) + 2]
                    window_sums(nc.gpsimd, hp[(KC * b + 2 * pair + 1) % 4], bufs, pair + 1, chain,
                                final=lambda ins: ins.then_inc(m_psum, 1))
                    if b == 1:
                        add_mixed(2 * pair)
                        add_mixed(2 * pair + 1)
            for r in range(8):
                add_squares(1, r)
            for c in range(KC):
                add_mixed(KC + c)
            for r in range(8, 16):
                add_squares(1, r)
            for r in range(16):
                add_squares(2, r)

            def times_cos(p):
                pool.wait_ge(rot_in[p % 2], 64 * (p // 2 + 1))
                nc.gpsimd.tensor_tensor(out=qg[p % 2][:, :], in0=qg[p % 2][:, :], in1=cos_t[:, :],
                                        op=ALU.mult).then_inc(p_cos, 1)

            pool.wait_ge(tables_in, 32)
            for p in range(N_PROJ):
                times_cos(p)

            def split_q(a):
                pool.wait_ge(p_done, N_PROJ * (a // 8) + KVH + a % 8 + 1)
                if a == 0:
                    pool.wait_ge(proj_done, N_PROJ)
                    pool.wait_ge(v_filled, 2)
                if a >= 2:
                    pool.wait_ge(s_filled, 4 * (a - 1))
                src = q_of(a % 8, a // 8)
                nc.gpsimd.tensor_scalar(qs_hi[:, a % 2, :], src, 1.0, 0.0, ALU.mult, ALU.add).then_inc(a_qhi, 1)
                pool.wait_ge(a_qhi, a + 1)
                nc.gpsimd.tensor_tensor(out=qs_lo[:, a % 2, :], in0=src, in1=qs_hi[:, a % 2, :].bitcast(F32),
                                        op=ALU.subtract).then_inc(a_q, 1)

            split_q(0)
            split_q(1)
            times_cos(N_PROJ)
            times_cos(N_PROJ + 1)
            for a in range(16):
                if a + 2 < 16:
                    split_q(a + 2)
                kind, n = BESIDE[a]
                if kind == "p":
                    times_cos(n)
                elif kind == "w" and n >= 1:
                    add_squares(3, n - 1)
                if a == 8:
                    pool.wait_ge(proj_done, NB * N_PROJ)
                    pool.wait_ge(o_copied, 8)
                    for h in range(6):
                        nc.gpsimd.tensor_scalar(o_hi[0][:, h, :], q_of(h, 0), 1.0, 0.0, ALU.mult,
                                                ALU.add).then_inc(o0_pool_hi, 1)
                        pool.wait_ge(o0_pool_hi, h + 1)
                        nc.gpsimd.tensor_tensor(out=o_lo[0][:, h, :], in0=q_of(h, 0),
                                                in1=o_hi[0][:, h, :].bitcast(F32), op=ALU.subtract
                                                ).then_inc(o0_pool, 1)
            for r in range(6, 16):
                add_squares(3, r)


def window_sums(eng, src, bufs, levels, chain, final=None):
    lo, hi, cur = 1, TP, src
    for level in range(levels):
        dst = bufs[level % 2]
        if level == 0:
            a, b = cur[:, 0:TP - 1], cur[:, 1:TP]
        else:
            s = 2 ** (level - 1)
            lo, hi = lo + s, hi - s
            a, b = cur[:, lo - s:hi - s], cur[:, lo + s:hi + s]
        ins = eng.tensor_tensor(out=dst[:, lo:hi], in0=a, in1=b, op=ALU.add)
        if level == levels - 1 and final is not None:
            final(ins)
        else:
            chain(ins)
        cur = dst
    return cur


def tables():
    import numpy as np
    grid_w, axis = 64, HD // 2
    t = np.arange(T)
    inv = (np.float32(10000.0) ** (-np.arange(0, axis, 2, dtype=np.float32) / np.float32(axis))).astype(np.float32)
    cos, sin = np.zeros((HD, T), np.float32), np.zeros((HD, T), np.float32)
    for d in range(HD):
        pos = (t // grid_w if d < axis else t % grid_w).astype(np.float32)
        ang = (pos * inv[d % 32]).astype(np.float32).astype(np.float64)
        cos[d] = np.cos(ang)
        sin[d] = np.sin(ang) * (-1.0 if d % axis < 32 else 1.0)
    edge = np.ones((P, len(WINDOWS), 2, EDGE), np.float32)
    for g, w in enumerate(WINDOWS):
        for side in range(2):
            for e in range(EDGE):
                tt = e if side == 0 else T - EDGE + e
                edge[:, g, side, e] = w / (min(tt + w // 2, T) - max(tt - w // 2, 0))
    return cos, sin, edge


_INS = ["x_prompt", "x_sample", "norm_mix", "norm_ffn", "pool_w", "pool_b", "pool_scale", "attn_w_qkv",
        "attn_q_gain", "attn_k_gain", "attn_w_o", "ffn_w_gate_up", "ffn_w_down"]


def kernel(**inputs):
    import numpy as np
    import concourse.bacc as bacc
    from concourse.bass_utils import run_bass_kernel_spmd as run

    nc = bacc.Bacc("TRN2", target_bir_lowering=False, num_devices=1)
    arrays, args = {}, []
    cos, sin, edge = tables()
    for name, a in [(n, np.ascontiguousarray(inputs[n])) for n in _INS] + [
            ("rope_cos", cos), ("rope_sin", sin), ("edge_tab", edge)]:
        arrays[f"in_{name}"] = a
        args.append(nc.dram_tensor(f"in_{name}", a.shape, mybir.dt.from_np(a.dtype), kind="ExternalInput").ap())
    for name in ("y_prompt", "y_sample"):
        args.append(nc.dram_tensor(f"out_{name}", (1, T, D), F32, kind="ExternalOutput").ap())
    build(nc, *args)
    r = run(nc, [arrays], core_ids=[0])
    return r.results[0]["out_y_prompt"], r.results[0]["out_y_sample"]
```

```python
from contextlib import ExitStack

import concourse.bass as bass
from concourse import mybir

F32 = mybir.dt.float32
F32R = mybir.dt.float32r
ALU = mybir.AluOpType
ACT = mybir.ActivationFunctionType
AX = mybir.AxisListType

P = 128
D = 1024
KC = D // P
T = 512
NB = 2
DFF = 2816
NF = DFF // P
GF = 2
NG = NF // GF
HEADS, KVH, HD = 8, 2, 128
EPS = 1e-6
WINDOWS = (2, 4, 8, 16)
NT = T // P
REACH = max(WINDOWS) // 2
BAND = P + 2 * REACH

UNIT = 1024
RAW = 3
RING = 6
U_POOL = 0
U_FFN0 = U_POOL + 2
N_FFN = NG * 3 * GF
N_QKV = 2 * KVH + HEADS
U_QKV = U_FFN0 + N_FFN
U_WO = U_QKV + NB * N_QKV
U_FFN1 = U_WO + NB * KC
U_FFN = (U_FFN0, U_FFN1)
N_TILE = NG * GF * NB
N_DOWN = NG * KC * NB
BODIES = 2
LOOPS = (NG - 2) // BODIES
FIRST_PEELED = 1 + LOOPS * BODIES
FIRST_TILE = (0, KC // 2)

N_PROJ = KVH + HEADS
N_PLAIN = N_PROJ + KVH
BESIDE = {-1: ("v", 1), 8: ("s", N_PLAIN + 7)}
BESIDE |= {a: ("p", N_PLAIN + a) for a in range(8)} | {a: ("w", a - 9) for a in range(9, 16)}
RING_WO = 4

V_MIX, V_FFN, V_PB, V_PS, V_QG, V_KG = 0, 16, 32, 40, 48, 49
N_VEC = 50
V_BS = 50


def build(nc, x_prompt, x_sample, norm_mix, norm_ffn, pool_w, pool_b, pool_scale, w_qkv, q_gain,
          k_gain, w_o, w_gu, w_down, rope_cos, rope_sin, band_tab, y_prompt, y_sample):
    with ExitStack() as ctx:
        base = (nc.sbuf_base + 31) // 32 * 32
        top = [base]

        def at(name, shape, dt, off):
            return nc.alloc_sbuf_tensor_at(name, shape, dt, offset=off)

        def take(nbytes):
            off = top[0]
            top[0] += nbytes
            return off

        o_x, o_h, o_act = take(KC * NB * T * 4), take(KC * NB * T * 8), take(32768)
        o_ring, o_raw, o_tmp = take(RING * UNIT * 8), take(RAW * UNIT * 4), take(8 * T * 4)
        o_const = take(0)
        x = at("x", [P, KC, NB * T], F32, o_x)
        half_hi = [at(f"half_hi{i}", [P, KC, T], F32R, o_h + 32768 * i) for i in range(2)]
        half_lo = [at(f"half_lo{i}", [P, KC, T], F32R, o_h + 32768 * i + 16384) for i in range(2)]
        act_hi = at("act_hi", [P, 2, GF, NB * T], F32R, o_act)
        act_lo = at("act_lo", [P, 2, GF, NB * T], F32R, o_act + 16384)
        k_hi = at("k_hi", [P, KVH, NB * T], F32R, o_act)
        k_lo = at("k_lo", [P, KVH, NB * T], F32R, o_act + 8192)
        v_hi = at("v_hi", [P, NB * T // P, KVH * HD], F32R, o_act + 16384)
        v_lo = at("v_lo", [P, NB * T // P, KVH * HD], F32R, o_act + 24576)
        band = at("band", [P, len(WINDOWS), 3, BAND], F32, o_act + 16384)
        w_hi_t = at("w_hi_t", [P, RING, UNIT], F32R, o_ring)
        w_lo_t = at("w_lo_t", [P, RING, UNIT], F32R, o_ring + RING * UNIT * 4)
        raw = at("raw", [P, RAW, UNIT], F32, o_raw)
        xin = [at("xin0", [P, NT, D], F32, o_h + 32768), at("xin1", [P, NT, D], F32, o_act)]
        xrms = [[at("xrms0_0", [P, 2, D], F32, o_h + 49152), at("xrms0_1", [P, 2, D], F32, o_h + 57344)],
                [at("xrms1_0", [P, 2, D], F32, o_ring + 2 * UNIT * 4),
                 at("xrms1_1", [P, 2, D], F32, o_ring + (RING + 2) * UNIT * 4)]]
        yout = at("yout", [P, NB * NT, D], F32, o_h)
        tmp = [at(f"tmp{i}", [P, T], F32, o_tmp + i * T * 4) for i in range(8)]
        scrap = at("scrap", [P, D], F32, o_tmp + 4 * T * 4)
        silu_t, full, sqr, stat = tmp[0:2], tmp[2:4], tmp[4:6], tmp[6:8]
        h_hi = {k: [half_hi[b if k < 3 else 1 - b] for b in range(NB)] for k in range(4)}
        h_lo = {k: [half_lo[b if k < 3 else 1 - b] for b in range(NB)] for k in range(4)}
        qg, rot, qsq, cos_t, sin_t = tmp[0:2], tmp[2:4], tmp[4:6], tmp[6], tmp[7]
        vec_in = at("vec_in", [N_VEC, P], F32, o_tmp)
        q_store = [[at(f"q_store{b}_{i}", [P, HEADS // 2, T], F32, o_ring + (i * RING + 2 + 2 * b) * UNIT * 4)
                    for i in range(2)] for b in range(NB)]
        prob = at("prob", [P, 4, T], F32, o_h)
        pt_hi = at("pt_hi", [P, 4, T], F32R, o_h + 8192)
        qs_hi = at("qs_hi", [P, 2, T], F32R, o_h + 16384)
        qs_lo = at("qs_lo", [P, 2, T], F32R, o_h + 20480)
        pt_lo = at("pt_lo", [P, 4, T], F32R, o_h + 24576)
        o_hi = [at("o_hi0", [P, HEADS, T], F32R, o_h + 32768), at("o_hi1", [P, HEADS, T], F32R, o_h)]
        o_lo = [at("o_lo0", [P, HEADS, T], F32R, o_h + 49152), at("o_lo1", [P, HEADS, T], F32R, o_h + 16384)]
        ident = at("ident", [P, P], F32, o_const)
        ones = at("ones", [P, P], F32, o_const + 512)
        vec = at("vec", [P, 64], F32, o_const + 1024)
        tok_rms = at("tok_rms", [P, NB * NT], F32, o_const + 1280)
        nmax = at("nmax", [P, 8], F32, o_const + 1536)
        rsum = at("rsum", [P, 8], F32, o_const + 1568)
        rinv = at("rinv", [P, 8], F32, o_const + 1600)
        epst = at("epst", [P, 2], F32, o_const + 1632)
        q_inv = at("q_inv", [P, NB * HEADS * T // P], F32, o_const + 1664)
        raw_max = at("raw_max", [P, 8], F32, o_const + 1920)
        assert o_const + 1952 <= nc.sbuf_usable_end, (o_const, nc.sbuf_usable_end)

        bank = [ctx.enter_context(nc.psum_tensor(f"bank{i}", [P, T], F32)) for i in range(8)]
        b_gate, b_up, b_down = bank[0:2], bank[2:4], bank[4:8]
        b_score, b_out, b_turn, b_side = bank[0:2], bank[2], bank[3:6], bank[6:8]

        def sem(name):
            return ctx.enter_context(nc.semaphore(name))

        x_in = [sem(f"x_in{i}") for i in range(NB * NT)]
        vec_landed, band_landed = sem("vec_landed"), sem("band_landed")
        ident_made, ones_made, eps_made = sem("ident_made"), sem("ones_made"), sem("eps_made")
        vec_turned, vec_ready = sem("vec_turned"), sem("vec_ready")
        t_sq, t_root, t_inv, t_norm = sem("t_sq"), sem("t_root"), sem("t_inv"), sem("t_norm")
        x_turned, x_moved, x_moved_dve = sem("x_turned"), sem("x_moved"), sem("x_moved_dve")
        raw_in = [sem(f"raw_in{i}") for i in range(RAW)]
        w_hi, w_lo = sem("w_hi"), sem("w_lo")
        n_sq, n_acc, n_ms, n_sqrt = sem("n_sq"), sem("n_acc"), sem("n_ms"), sem("n_sqrt")
        n_rstd, n_full, n_hi, n_lo = sem("n_rstd"), sem("n_full"), sem("n_hi"), sem("n_lo")
        m_band, m_hi, m_lo, m_filled, m_x = sem("m_band"), sem("m_hi"), sem("m_lo"), sem("m_filled"), sem("m_x")
        gate_done, up_done, silu_done, prod_done = sem("gate_done"), sem("up_done"), sem("silu_done"), sem("prod_done")
        act_hi_done, act_lo_done = sem("act_hi_done"), sem("act_lo_done")
        down_filled, down_added = sem("down_filled"), sem("down_added")
        proj_done, p_sq, p_gain, p_ms, p_sqrt = sem("proj_done"), sem("p_sq"), sem("p_gain"), sem("p_ms"), sem("p_sqrt")
        rot_in = [sem("rot_in0"), sem("rot_in1")]
        p_r, p_cos, p_sin, p_sum, p_fin, p_hi, p_done = (sem("p_r"), sem("p_cos"), sem("p_sin"), sem("p_sum"),
                                                        sem("p_fin"), sem("p_hi"), sem("p_done"))
        v_half = sem("v_half")
        v_filled, v_hi_done, v_lo_done, tables_in = sem("v_filled"), sem("v_hi_done"), sem("v_lo_done"), sem("tables_in")
        a_qhi, a_q, s_filled, a_max, a_exp = sem("a_qhi"), sem("a_q"), sem("s_filled"), sem("a_max"), sem("a_exp")
        a_rawmax = sem("a_rawmax")
        a_rinv, a_prob, pt_filled, a_pthi, a_ptlo = sem("a_rinv"), sem("a_prob"), sem("pt_filled"), sem("a_pthi"), sem("a_ptlo")
        o_filled, o_copied = sem("o_filled"), sem("o_copied")
        o0_pool_hi, o0_pool = sem("o0_pool_hi"), sem("o0_pool")
        o0_hi, o0_split, o1_hi, o1_split = sem("o0_hi"), sem("o0_split"), sem("o1_hi"), sem("o1_split")
        wo_filled, wo_added = sem("wo_filled"), sem("wo_added")
        y_turned, y_act, y_dve, y_out = sem("y_turned"), sem("y_act"), sem("y_dve"), sem("y_out")

        block = ctx.enter_context(nc.Block())

        def tok(b):
            return slice(b * T, (b + 1) * T)

        def slot(u):
            if U_QKV <= u < U_WO:
                return (u - U_QKV) % 2
            if U_WO <= u < U_FFN1:
                return (u - U_WO) % RING_WO
            if u >= U_FFN1:
                return (u - U_FFN1) % RING
            return (u - U_FFN0) % RING

        def gu_unit(layer, g, c, up):
            return U_FFN[layer] + (0 if g == 0 else 4 + 6 * (g - 1)) + 2 * c + up

        def down_unit(layer, g, c):
            return U_FFN[layer] + (4 + 6 * g + 4 if g < NG - 1 else N_FFN - 2) + c

        def q_of(h, b):
            return q_store[b][h // 4][:, h % 4, :]

        gu_rows = [w_gu[l].rearrange("(k p) f -> p k f", p=P) for l in range(2)]
        qkv_rows = w_qkv[0].rearrange("(k p) e -> p k e", p=P)
        wo_rows = w_o[0].rearrange("(k p) e -> p k e", p=P)

        @block.sync
        def _(sp):
            def load_unit(u, src, shape, w_lo_before=None):
                if w_lo_before is not None:
                    sp.wait_ge(w_lo, w_lo_before)
                elif u >= RAW:
                    sp.wait_ge(w_lo, u - RAW + 1)
                dst = raw[:, u % RAW, :]
                if shape:
                    dst = dst.rearrange("p (k f) -> p k f", k=shape)
                sp.dma_start(dst, src).then_inc(raw_in[u % RAW], 16)

            def load_gu(layer, g, j=None, g0=None):
                for c in range(GF):
                    for up in range(2):
                        u = gu_unit(layer, g if j is None else g0, c, up)
                        if j is None:
                            col = up * DFF + (GF * g + c) * P
                            load_unit(u, gu_rows[layer][:, :, col:col + P], KC)
                        else:
                            col = j * (BODIES * GF * P) + up * DFF + (GF * g0 + c) * P
                            load_unit(u, gu_rows[layer][:, :, bass.ds(col, P)], KC,
                                      j * (6 * BODIES) + u - RAW + 1)

            def load_down(layer, g, j=None, g0=None):
                for c in range(GF):
                    u = down_unit(layer, g if j is None else g0, c)
                    if j is None:
                        r = (GF * g + c) * P
                        load_unit(u, w_down[layer][r:r + P, :], 0)
                    else:
                        r = j * (BODIES * GF * P) + (GF * g0 + c) * P
                        load_unit(u, w_down[layer][bass.ds(r, P), :], 0, j * (6 * BODIES) + u - RAW + 1)

            def load_ffn(layer):
                load_gu(layer, 0)
                with sp.Fori(0, LOOPS) as j:
                    for g0 in range(1, 1 + BODIES):
                        load_gu(layer, None, j, g0)
                        load_down(layer, None, j, g0 - 1)
                for g in range(FIRST_PEELED, NG):
                    load_gu(layer, g)
                    load_down(layer, g - 1)
                load_down(layer, NG - 1)

            def load_x(b):
                for i in range(NT):
                    sp.dma_start(xin[b][:, i, :], (x_prompt, x_sample)[b][0][i * P:(i + 1) * P, :]
                                 ).then_inc(x_in[NT * b + i], 16)

            load_x(0)
            for row, src in ((V_MIX, norm_mix.rearrange("l (c p) -> (l c) p", p=P)),
                             (V_FFN, norm_ffn.rearrange("l (c p) -> (l c) p", p=P)),
                             (V_PB, pool_b.rearrange("l g (c p) -> (l g c) p", p=P)),
                             (V_PS, pool_scale.rearrange("l (c p) -> (l c) p", p=P)),
                             (V_QG, q_gain), (V_KG, k_gain)):
                sp.dma_start(vec_in[row:row + src.shape[0], :], src).then_inc(vec_landed, 16)
            sp.dma_start(band[:, :, :, :], band_tab).then_inc(band_landed, 16)
            for i in range(2):
                sp.dma_start(raw[:, i, :].rearrange("p (g k e) -> p g k e", g=2, k=2),
                             pool_w[0, 2 * i:2 * i + 2].rearrange("g (k p) e -> p g k e", p=P)
                             ).then_inc(raw_in[i], 16)
            load_x(1)
            load_ffn(0)

            def load_qkv(b, i):
                u = U_QKV + N_QKV * b + i
                if i < 2:
                    load_unit(u, qkv_rows[:, :, (HEADS + i) * HD:(HEADS + i + 1) * HD], KC)
                elif i < 4:
                    k0 = (i - 2) * 4
                    load_unit(u, qkv_rows[:, k0:k0 + 4, (HEADS + KVH) * HD:], 4)
                else:
                    load_unit(u, qkv_rows[:, :, (i - 4) * HD:(i - 3) * HD], KC)

            def load_attention(i):
                if i < NB * N_QKV:
                    load_qkv(i // N_QKV, i % N_QKV)
                elif U_QKV + i < U_FFN1:
                    m = (i - NB * N_QKV) % KC
                    load_unit(U_QKV + i, wo_rows[:, :, m * P:(m + 1) * P], KC)

            def rotate(p):
                sp.wait_ge(p_gain, p + 1)
                for dst, src in ((0, 1), (1, 0), (2, 3), (3, 2)):
                    sp.dma_start(rot[p % 2][32 * dst:32 * dst + 32, :],
                                 qg[p % 2][32 * src:32 * src + 32, :]).then_inc(rot_in[p % 2], 16)

            for i in range(RAW):
                load_attention(i)
            for i in range(NB * N_QKV):
                load_attention(i + RAW)
                b, j = i // N_QKV, i % N_QKV
                if i == 2:
                    sp.wait_ge(n_lo, 2 * 16)
                    sp.dma_start(cos_t[:, :], rope_cos).then_inc(tables_in, 16)
                    sp.dma_start(sin_t[:, :], rope_sin).then_inc(tables_in, 16)
                    for p in range(KVH):
                        rotate(p)
                elif b == 1 and j < 2:
                    rotate(N_PROJ * b + j)
                elif j >= 4:
                    rotate(N_PROJ * b + j - 2)
            for i in range(NB * N_QKV + RAW, U_FFN1 - U_QKV):
                load_attention(i)
            load_ffn(1)

            for i in range(NB * T // P):
                sp.wait_ge(y_act, i + 1)
                sp.wait_ge(y_dve, i + 1)
                dst = (y_prompt, y_sample)[i // 4][0]
                r = (i % 4) * P
                sp.dma_start(dst[r:r + P, :], yout[:, i, :]).then_inc(y_out, 16)
            sp.wait_ge(y_out, 16 * (NB * T // P))

        SEQ = [(c, b) for b in range(NB) for c in range(KC)]
        GAIN = {1: V_FFN, 2: V_MIX + KC, 3: V_FFN + KC}

        def acc_index(k, r):
            return 14 * (k - 1) + sum(1 for c, _ in SEQ[:r + 1] if c > 0)

        def wait_unit_used(eng, i):
            b, j = i // N_QKV, i % N_QKV
            if i >= NB * N_QKV:
                eng.wait_ge(wo_filled, i - NB * N_QKV + 1)
            elif j == 2:
                eng.wait_ge(v_half, b + 1)
            elif j == 3:
                eng.wait_ge(v_filled, 2 * (b + 1))
            else:
                eng.wait_ge(proj_done, N_PROJ * b + (j if j < 2 else j - 2) + 1)

        def following(i):
            return U_QKV + i + (2 if U_QKV + i < U_WO else RING_WO)

        def unit_of(kind, n):
            if kind == "w":
                return NB * N_QKV + n
            j = n % N_PROJ
            return N_QKV * (n // N_PROJ) + (j if j < 2 else j + 2)

        def q_cols(p):
            a = HEADS * (p // N_PROJ) + p % N_PROJ - KVH
            return slice(T // P * a, T // P * (a + 1))

        @block.tensor
        def _(pe):
            def product(out, parts, first, last, done=None):
                n = len(parts)
                for i, (w, m) in enumerate(parts):
                    ins = pe.matmul(out, w, m, start=first and i == 0, stop=last and i == n - 1)
                if done is not None:
                    ins.then_inc(done, 1)

            def three(whi, wlo, mhi, mlo):
                return [(whi, mhi), (whi, mlo), (wlo, mhi)]

            def w_chunk(u, k):
                return w_hi_t[:, slot(u), k * P:(k + 1) * P], w_lo_t[:, slot(u), k * P:(k + 1) * P]

            def mean_square(k, b, out):
                r = max(i for i, (_, bb) in enumerate(SEQ) if bb == b)
                pe.wait_ge(n_acc, acc_index(k, r))
                pe.matmul(out[:, :], ones[:, :], stat[b][:, :], start=True, stop=True).then_inc(n_ms, 1)

            pe.wait_ge(ident_made, 2)

            def turn_x(b):
                for i in range(NT):
                    pe.wait_ge(x_in[NT * b + i], 16)
                for c in range(KC):
                    q = KC * b + c
                    if b == 0 and c == 4:
                        pe.wait_ge(vec_landed, 6 * 16)
                        pe.transpose(bank[0][:, 0:N_VEC], vec_in[:, :], ident[0:N_VEC, 0:N_VEC]
                                     ).then_inc(vec_turned, 1)
                    if b == 1 and c < 4:
                        pe.wait_ge(m_x, 4 + c + 1)
                    elif c >= 4:
                        pe.wait_ge(x_moved, 4 * b + c - 3)
                    for i in range(NT):
                        ins = pe.transpose(b_down[c % 4][:, i * P:(i + 1) * P], xin[b][:, i, c * P:(c + 1) * P],
                                           ident[:, :])
                    ins.then_inc(x_turned, 1)

            def pool(b, c):
                q = KC * b + c
                if q >= 3:
                    pe.wait_ge(m_lo, q - 2)
                elif q == 0:
                    pe.wait_ge(vec_ready, 1)
                for i in range(NT):
                    if c == 0:
                        pe.wait_ge(t_norm, NT * b + i + 1)
                    first, last = max(i * P - REACH, 0), min((i + 1) * P + REACH, T)
                    kind = 0 if i == 0 else 2 if i == NT - 1 else 1
                    ins = pe.matmul(bank[q % 3][:, first:last], xrms[b][i // 2][:, i % 2, c * P:(c + 1) * P],
                                    band[:, c // 2, kind, 0:last - first], start=i == 0, stop=i == NT - 1,
                                    skip_group_check=True)
                ins.then_inc(m_band, 1)

            def mix(b, g):
                pe.wait_ge(w_lo, g // 2 + 1)
                pe.wait_ge(m_lo, KC * b + 2 * g + 2)
                for m in range(2):
                    q = KC * b + 2 * g + m
                    if 2 * g + m >= 4:
                        pe.wait_ge(m_x, q - 3)
                    elif g == 0 and m == 0:
                        pe.wait_ge(x_moved, KC * b + 4)
                        pe.wait_ge(x_moved_dve, 4)
                    parts = []
                    for k in range(2):
                        lo = (g % 2) * 512 + k * 256 + m * P
                        s = slot(g // 2)
                        parts += three(w_hi_t[:, s, lo:lo + P], w_lo_t[:, s, lo:lo + P],
                                       h_hi[0][b][:, 2 * g + k, :], h_lo[0][b][:, 2 * g + k, :])
                    product(b_down[q % 4][:, :], parts, True, True, m_filled)

            turn_x(0)
            pe.wait_ge(band_landed, 16)
            for b in range(NB):
                for c in range(3):
                    pool(b, c)
                if b == 1:
                    mean_square(1, 0, bank[3])
                    turn_x(1)
                pool(b, 3)
                mix(b, 0)
                pool(b, 4)
                pool(b, 5)
                mix(b, 1)
                pool(b, 6)
                pool(b, 7)
                mix(b, 2)
                mix(b, 3)

            def gate_up_half(layer, g, c, b, up, t, norm=None):
                u = gu_unit(layer, g, c, up)
                out = (b_up if up else b_gate)[t % 2]
                for k in range(KC):
                    whi, wlo = w_chunk(u, k)
                    hk = 2 * layer + 1
                    parts = three(whi, wlo, h_hi[hk][b][:, k, :], h_lo[hk][b][:, k, :])
                    if norm is not None:
                        pe.wait_ge(n_lo, (norm - 1) * 16 + KC * b + k + 1)
                    product(out[:, :], parts, k == 0, k == KC - 1,
                            None if k < KC - 1 else (up_done if up else gate_done))

            def tile(layer, g, t, j=None, norm=None, between=None):
                c, b = t % 2, t // 2
                n = N_TILE * layer + 4 * g + t
                step = 0 if j is None else j * (4 * BODIES)
                ustep = 0 if j is None else j * (6 * BODIES)
                if 4 * g + t >= 2:
                    pe.wait_ge(prod_done, step + n - 1)
                for up in range(2):
                    if b == 0:
                        pe.wait_ge(w_lo, ustep + gu_unit(layer, g, c, up) + 1)
                    gate_up_half(layer, g, c, b, up, t, norm if up == 0 and c == 0 else None)
                    if between is not None and up == 0:
                        between()

            def down_bank(layer, g, b, m, j=None):
                i = KC * b + m
                q = N_DOWN * layer + 16 * g + i
                step = 0 if j is None else j * (16 * BODIES)
                if 16 * g + i >= 4:
                    pe.wait_ge(down_added, step + q - 3)
                parts = []
                for c in range(GF):
                    whi, wlo = w_chunk(down_unit(layer, g, c), m)
                    parts += three(whi, wlo, act_hi[:, g % 2, c, tok(b)], act_lo[:, g % 2, c, tok(b)])
                product(b_down[i % 4][:, :], parts, True, True, down_filled)

            def down(layer, g, j=None):
                tstep = 0 if j is None else j * (4 * BODIES)
                ustep = 0 if j is None else j * (6 * BODIES)
                pe.wait_ge(w_lo, ustep + down_unit(layer, g, 1) + 1)
                pe.wait_ge(act_lo_done, tstep + N_TILE * layer + 4 * (g + 1))
                for b in range(NB):
                    for m in range(KC):
                        down_bank(layer, g, b, m, j)

            def swiglu(layer, norm, ms_b1):
                for t in range(4):
                    if layer == 0 and t == 1:
                        ms_b1()
                    tile(layer, 0, t, norm=norm, between=ms_b1 if layer == 1 and t == 0 else None)
                with pe.Fori(0, LOOPS) as j:
                    for g in range(1, 1 + BODIES):
                        for t in range(4):
                            tile(layer, g, t, j)
                        down(layer, g - 1, j)
                for g in range(FIRST_PEELED, NG):
                    for t in range(4):
                        tile(layer, g, t)
                    down(layer, g - 1)

            def turn_y(b):
                for q in range(2 * NT * b, 2 * NT * (b + 1)):
                    i, half = q // 2, q % 2
                    if q % 8 == 0:
                        pe.wait_ge(down_added, N_DOWN * 2 - 8 + q)
                    if q >= 4:
                        if half == 0:
                            pe.wait_ge(y_act, q // 2 - 1)
                        else:
                            pe.wait_ge(y_dve, q // 2 - 1)
                    for c in range(4):
                        ins = pe.transpose(bank[q % 4][:, c * P:(c + 1) * P],
                                           x[:, 4 * half + c, i * P:(i + 1) * P], ident[:, :])
                    ins.then_inc(y_turned, 1)

            def down_last(layer, inside):
                g = NG - 1
                pe.wait_ge(w_lo, down_unit(layer, g, 1) + 1)
                pe.wait_ge(act_lo_done, N_TILE * (layer + 1))
                for b in range(NB):
                    for m in range(KC):
                        down_bank(layer, g, b, m)
                        if b == 1 and m == 2 and inside is not None:
                            inside()

            swiglu(0, 1, lambda: mean_square(1, 1, b_down[0]))
            down_last(0, lambda: mean_square(2, 0, bank[1]))

            def project(p, out, bank_free, quarter=None):
                b, u = p // N_PROJ, U_QKV + unit_of("p", p)
                if quarter in (None, 0):
                    if bank_free > 0:
                        pe.wait_ge(p_gain, bank_free)
                    pe.wait_ge(w_lo, u + 1)
                for k in range(KC) if quarter is None else range(2 * quarter, 2 * quarter + 2):
                    whi, wlo = w_chunk(u, k)
                    if p == 0:
                        pe.wait_ge(n_lo, 16 + k + 1)
                    product(out[:, :], three(whi, wlo, h_hi[2][b][:, k, :], h_lo[2][b][:, k, :]),
                            k == 0, k == KC - 1, proj_done if k == KC - 1 else None)
                    if k == 1 and p > 0 and p not in (KVH, N_PLAIN):
                        if p < N_PLAIN:
                            head_square(p - 1, b_up[(p - 1) % 2], p - 2)
                        else:
                            head_square(p - 1, b_side[1], p - 1)

            def head_square(p, out, bank_free):
                pe.wait_ge(p_sq, p + 1)
                if bank_free > 0:
                    pe.wait_ge(p_sqrt, bank_free)
                if p % N_PROJ >= KVH:
                    for i in range(T // P):
                        ins = pe.matmul(out[:, i:i + 1], qsq[p % 2][:, i * P:(i + 1) * P], ones[:, 0:1],
                                        start=True, stop=True)
                    ins.then_inc(p_ms, 1)
                    return
                pe.matmul(out[:, :], ones[:, :], qsq[p % 2][:, :], start=True, stop=True).then_inc(p_ms, 1)

            def values(b, banks, quarter):
                half = quarter // 2
                u = U_QKV + N_QKV * b + 2 + half
                if quarter % 2 == 0:
                    pe.wait_ge(w_lo, u + 1)
                for t in range(2 * (quarter % 2), 2 * (quarter % 2) + 2):
                    parts = []
                    for k in range(4 * half, 4 * half + 4):
                        c0 = (k % 4) * 256
                        hh = h_hi[2][b][:, k, t * P:(t + 1) * P]
                        hl = h_lo[2][b][:, k, t * P:(t + 1) * P]
                        wh, wl = w_hi_t[:, slot(u), c0:c0 + 256], w_lo_t[:, slot(u), c0:c0 + 256]
                        parts += [(hh, wh), (hh, wl), (hl, wh)]
                    out = banks[t // 2][:, (t % 2) * 256:(t % 2) * 256 + 256]
                    for i, (w, m) in enumerate(parts):
                        ins = pe.matmul(out, w, m, start=half == 0 and t % 2 == 0 and i == 0,
                                        stop=half == 1 and i == len(parts) - 1, skip_group_check=True)
                    if half == 0 and t == 3:
                        ins.then_inc(v_half, 1)
                    if half == 1 and t % 2 == 1:
                        ins.then_inc(v_filled, 1)

            project(0, b_gate[0], 0)
            mean_square(2, 1, b_down[3])
            project(1, b_gate[1], 0)
            for quarter in range(4):
                values(0, b_down[0:2], quarter)
                if quarter == 1:
                    head_square(1, b_up[1], 0)
            for p in range(KVH, N_PLAIN):
                project(p, b_gate[p % 2], p - 1)

            def score(a, i):
                b, kv = a // 8, a % 8 // 4
                if i == 0:
                    pe.wait_ge(a_q, a + 1)
                s = 4 * a + i
                if s >= 2:
                    pe.wait_ge(a_exp, s - 1)
                c = slice(i * P, (i + 1) * P)
                product(b_score[s % 2][:, :],
                        three(qs_hi[:, a % 2, c], qs_lo[:, a % 2, c], k_hi[:, kv, tok(b)], k_lo[:, kv, tok(b)]),
                        True, True, s_filled)

            def turn_probs(a, tiles):
                pe.wait_ge(a_prob, 4 * a + 4)
                for sc in tiles:
                    r = 4 * a + sc
                    if r >= 3:
                        pe.wait_ge(a_ptlo, r - 2)
                    for i in range(4):
                        ins = pe.transpose(b_turn[r % 3][:, i * P:(i + 1) * P], prob[:, i, sc * P:(sc + 1) * P],
                                           ident[:, :])
                    ins.then_inc(pt_filled, 1)

            def attend(a):
                b, kv = a // 8, a % 8 // 4
                if a >= 1:
                    pe.wait_ge(o_copied, a)
                for sc in range(4):
                    pe.wait_ge(a_ptlo, 4 * a + sc + 1)
                    t, c = 4 * b + sc, slice(kv * HD, (kv + 1) * HD)
                    product(b_out[:, :], three(v_hi[:, t, c], v_lo[:, t, c], pt_hi[:, sc, :], pt_lo[:, sc, :]),
                            sc == 0, sc == 3, o_filled if sc == 3 else None)

            def project_out(w, quarter=None):
                b, u = w // KC, U_WO + w
                if quarter in (None, 0):
                    pe.wait_ge(w_lo, u + 1)
                    if w >= 2:
                        pe.wait_ge(wo_added, w - 1)
                    else:
                        pe.wait_ge(p_sqrt, NB * N_PROJ)
                for k in range(HEADS) if quarter is None else range(2 * quarter, 2 * quarter + 2):
                    if w == KC:
                        pe.wait_ge(o1_split, k + 1)
                    elif w == 0:
                        pe.wait_ge(o0_pool if k < 6 else o0_split, k % 6 + 1)
                    whi, wlo = w_chunk(u, k)
                    product(b_side[w % 2][:, :], three(whi, wlo, o_hi[b][:, k, :], o_lo[b][:, k, :]),
                            k == 0, k == HEADS - 1, wo_filled if k == HEADS - 1 else None)

            def beside(a, i):
                kind, n = BESIDE[a]
                if kind == "p":
                    if a == 0 and i == 0:
                        pe.wait_ge(v_lo_done, 4)
                    project(n, b_side[0], n, i)
                elif kind == "v":
                    values(1, b_side, i)
                elif kind == "w":
                    project_out(n, i)
                elif i == 0:
                    head_square(n, b_side[1], n)

            beside(-1, 0)
            head_square(N_PLAIN - 1, b_up[1], N_PLAIN - 2)
            beside(-1, 1)
            pe.wait_ge(p_gain, N_PLAIN)
            for i in range(4):
                score(0, i)
                if i in (1, 3):
                    beside(-1, 2 + i // 2)
            pe.wait_ge(p_sqrt, N_PLAIN)
            pe.wait_ge(v_lo_done, 2)
            for a in range(16):
                turn_probs(a, range(3))
                for i in range(4):
                    beside(a, i)
                    if a + 1 < 16:
                        score(a + 1, i)
                    if i == 0:
                        turn_probs(a, [3])
                attend(a)

            for w in range(7, 16):
                project_out(w)
                if w == 9:
                    mean_square(3, 0, bank[1])
            swiglu(1, 3, lambda: mean_square(3, 1, b_down[0]))
            down_last(1, lambda: turn_y(0))

            turn_y(1)

        @block.scalar
        def _(act):
            def split_hi(u, step=None):
                if step is None:
                    act.wait_ge(raw_in[u % RAW], 16 * (u // RAW + 1))
                else:
                    act.wait_ge(raw_in[u % RAW], step * (16 * 6 * BODIES // RAW) + 16 * (u // RAW + 1))
                nc.scalar.copy(w_hi_t[:, slot(u), :], raw[:, u % RAW, :]).then_inc(w_hi, 1)

            def square(k, r, ready):
                c, b = SEQ[r]
                ready(c, b)
                if c == 0:
                    dst = stat[b]
                else:
                    i = acc_index(k, r)
                    if i > 2:
                        act.wait_ge(n_acc, i - 2)
                    dst = sqr[i % 2]
                nc.scalar.activation(dst[:, :], x[:, c, tok(b)], ACT.Square).then_inc(n_sq, 1)

            def root(k, b, src):
                act.wait_ge(n_ms, 2 * (k - 1) + b + 1)
                nc.scalar.activation(stat[b][:, :], src[:, :], ACT.Sqrt, bias=epst[:, 0:1],
                                     scale=1.0 / D).then_inc(n_sqrt, 1)

            def norm_hi(k, b, c):
                i = 16 * (k - 1) + KC * b + c
                act.wait_ge(n_full, i + 1)
                nc.scalar.copy(h_hi[k][b][:, c, :], full[i % 2][:, :]).then_inc(n_hi, 1)

            act.wait_ge(eps_made, 2)

            def token_root(b):
                for i in range(NT * b, NT * (b + 1)):
                    act.wait_ge(x_in[i], 16)
                    if i > 0:
                        act.wait_ge(t_sq, i)
                    nc.scalar.activation(scrap[:, :], xin[b][:, i % NT, :], ACT.Square,
                                         accum_out=tok_rms[:, i:i + 1]).then_inc(t_sq, 1)
                act.wait_ge(t_sq, NT * (b + 1))
                cols = tok_rms[:, NT * b:NT * (b + 1)]
                nc.scalar.activation(cols, cols, ACT.Sqrt, bias=epst[:, 0:1], scale=1.0 / D).then_inc(t_root, 1)

            def move_x(b, c):
                act.wait_ge(x_turned, KC * b + c + 1)
                nc.scalar.activation(x[:, c, tok(b)], b_down[c % 4][:, :], ACT.Identity,
                                     bias=vec[:, V_BS + c:V_BS + c + 1]).then_inc(x_moved, 1)

            def pooled_hi(b, c):
                q = KC * b + c
                act.wait_ge(m_band, q + 1)
                nc.scalar.copy(h_hi[0][b][:, c, :], bank[q % 3][:, :]).then_inc(m_hi, 1)

            def x_mixed(c, b):
                act.wait_ge(m_x, KC * b + c + 1)

            def gained_hi(u):
                act.wait_ge(raw_in[u], 16)
                for j in range(4):
                    blk = slice(256 * j, 256 * (j + 1))
                    ins = nc.scalar.activation(w_hi_t[:, slot(u), blk], raw[:, u, blk], ACT.Copy,
                                               scale=vec[:, V_MIX + 4 * u + j:V_MIX + 4 * u + j + 1])
                ins.then_inc(w_hi, 1)

            token_root(0)
            act.wait_ge(vec_ready, 2)
            for c in range(4):
                move_x(0, c)
            pooled_hi(0, 0)
            pooled_hi(0, 1)
            gained_hi(0)
            pooled_hi(0, 2)
            pooled_hi(0, 3)
            gained_hi(1)
            token_root(1)
            pooled_hi(0, 4)
            pooled_hi(0, 5)
            square(1, 0, x_mixed)
            square(1, 1, x_mixed)
            split_hi(U_FFN0)
            pooled_hi(0, 6)
            pooled_hi(0, 7)
            square(1, 2, x_mixed)
            square(1, 3, x_mixed)
            split_hi(U_FFN0 + 1)
            for r in range(4, 8):
                square(1, r, x_mixed)
            for c in range(3):
                pooled_hi(1, c)
            root(1, 0, bank[3])
            for c in range(KC):
                move_x(1, c)
            pooled_hi(1, 3)
            for c in (0, 2):
                norm_hi(1, 0, c)
                norm_hi(1, 0, c + 1)
                pooled_hi(1, 4 + c)
                pooled_hi(1, 5 + c)
            square(1, 8, x_mixed)
            square(1, 9, x_mixed)
            for c in (4, 6):
                norm_hi(1, 0, c)
                norm_hi(1, 0, c + 1)
                square(1, 6 + c, x_mixed)
                square(1, 7 + c, x_mixed)
            square(1, 14, x_mixed)
            square(1, 15, x_mixed)
            split_hi(U_FFN0 + 2)
            split_hi(U_FFN0 + 3)
            act.wait_ge(m_filled, 16)
            split_hi(U_FFN0 + 4)
            root(1, 1, b_down[0])
            split_hi(U_FFN0 + 5)
            def silu(layer, g, t, j=None):
                i = 4 * g + t
                n = N_TILE * layer + i
                step = 0 if j is None else j * (4 * BODIES)
                act.wait_ge(gate_done, step + n + 1)
                if i >= 2:
                    act.wait_ge(prod_done, step + n - 1)
                nc.scalar.activation(silu_t[t % 2][:, :], b_gate[t % 2][:, :], ACT.Silu).then_inc(silu_done, 1)

            def hidden_hi(layer, g, t, j=None):
                c, b = t % 2, t // 2
                step = 0 if j is None else j * (4 * BODIES)
                act.wait_ge(prod_done, step + N_TILE * layer + 4 * g + t + 1)
                nc.scalar.copy(act_hi[:, g % 2, c, tok(b)], full[t % 2][:, :]).then_inc(act_hi_done, 1)

            def group(layer, g, j=None):
                tstep = 0 if j is None else j * (4 * BODIES)
                dstep = 0 if j is None else j * (16 * BODIES)
                for t in range(4):
                    if g == 0 and t == 0:
                        for c in range(FIRST_TILE[layer]):
                            norm_hi(2 * layer + 1, 1, c)
                    silu(layer, g, t, j)
                    hidden_hi(layer, g, t, j)
                    if g == 0 and t == 0:
                        for c in range(FIRST_TILE[layer], KC):
                            norm_hi(2 * layer + 1, 1, c)
                    if t >= 2:
                        act.wait_ge(up_done, tstep + N_TILE * layer + 4 * g + t + 1)
                        for up in range(2):
                            u = gu_unit(layer, g, t - 2, up) + RING
                            if u < U_FFN[layer] + N_FFN or (layer == 0 and slot(u) < 2):
                                split_hi(u, j)
                if g >= 1 and down_unit(layer, g - 1, 0) + RING < U_FFN[layer] + N_FFN:
                    act.wait_ge(down_filled, dstep + N_DOWN * layer + 16 * g)
                    for c in range(GF):
                        split_hi(down_unit(layer, g - 1, c) + RING, j)

            def swiglu(layer):
                group(layer, 0)
                with act.Fori(0, LOOPS) as j:
                    for g in range(1, 1 + BODIES):
                        group(layer, g, j)
                for g in range(FIRST_PEELED, NG):
                    group(layer, g)

            swiglu(0)

            def x_ffn0(c, b):
                act.wait_ge(down_added, N_DOWN - 16 + KC * b + c + 1)

            for r in range(8):
                square(2, r, x_ffn0)
            root(2, 0, bank[1])
            for c in range(KC):
                square(2, 8 + c, x_ffn0)
                norm_hi(2, 0, c)

            def gain(p, src):
                act.wait_ge(proj_done, p + 1)
                if p >= 2:
                    act.wait_ge(p_done, p - 1)
                    act.wait_ge(p_ms, p - 1)
                else:
                    act.wait_ge(n_acc, 2 * 14)
                g = V_KG if p % N_PROJ < KVH else V_QG
                nc.scalar.activation(qsq[p % 2][:, :], src[:, :], ACT.Square).then_inc(p_sq, 1)
                nc.scalar.activation(qg[p % 2][:, :], src[:, :], ACT.Copy,
                                     scale=vec[:, g:g + 1]).then_inc(p_gain, 1)

            def head_root(p, src):
                act.wait_ge(p_ms, p + 1)
                if p % N_PROJ < KVH:
                    nc.scalar.activation(qsq[p % 2][:, :], src[:, :], ACT.Sqrt, bias=epst[:, 0:1],
                                         scale=1.0 / HD).then_inc(p_sqrt, 1)
                else:
                    nc.scalar.activation(q_inv[:, q_cols(p)], src[:, 0:T // P], ACT.Sqrt,
                                         bias=epst[:, 1:2]).then_inc(p_sqrt, 1)

            def key_hi(p):
                b, j = p // N_PROJ, p % N_PROJ
                act.wait_ge(p_fin, KVH * b + j + 1)
                nc.scalar.copy(k_hi[:, j, tok(b)], rot[p % 2][:, :]).then_inc(p_hi, 1)

            def split_next(i):
                wait_unit_used(act, i)
                split_hi(following(i))

            def values_hi(b, banks):
                for t in range(2):
                    act.wait_ge(v_filled, 2 * b + t + 1)
                    nc.scalar.copy(v_hi[:, 4 * b + 2 * t:4 * b + 2 * t + 2, :],
                                   banks[t][:, :].rearrange("p (t f) -> p t f", t=2)).then_inc(v_hi_done, 1)

            gain(0, b_gate[0])
            split_next(0)
            root(2, 1, b_down[3])
            for c in range(4):
                norm_hi(2, 1, c)
            head_root(0, b_up[0])
            gain(1, b_gate[1])
            split_next(1)
            for c in range(4, KC):
                norm_hi(2, 1, c)
            head_root(1, b_up[1])
            split_next(2)
            split_next(3)
            key_hi(0)
            gain(2, b_gate[0])
            key_hi(1)
            values_hi(0, b_down)
            split_next(4)
            for p in range(3, N_PLAIN):
                gain(p, b_gate[p % 2])
                split_next(unit_of("p", p))
                head_root(p - 1, b_up[(p - 1) % 2])

            def exps(a, tiles=range(4)):
                for i in tiles:
                    s = 4 * a + i
                    act.wait_ge(a_max, s + 1)
                    if a >= 1:
                        act.wait_ge(pt_filled, 4 * a)
                    else:
                        act.wait_ge(proj_done, N_PROJ)
                    nc.scalar.activation(prob[:, i, :], b_score[s % 2][:, :], ACT.Exp, bias=nmax[:, s % 8:s % 8 + 1], scale=q_inv[:, s:s + 1],
                                         accum_out=rsum[:, s % 8:s % 8 + 1]).then_inc(a_exp, 1)

            def x_attn(c, b):
                act.wait_ge(wo_added, KC * b + c + 1)
                if c == 0 and b == 0:
                    act.wait_ge(p_cos, NB * N_PROJ)
                    act.wait_ge(p_done, NB * N_PROJ)

            def splits_after(a):
                if 0 <= a < 8:
                    split_next(unit_of(*BESIDE[a]))
                elif a == 9:
                    split_hi(U_WO + 3)
                elif a >= 10:
                    split_next(unit_of("w", a - 10))

            head_root(N_PLAIN - 1, b_up[1])
            exps(0)
            split_next(N_QKV + 2)
            values_hi(1, b_side)
            split_next(N_QKV + 3)
            key_hi(N_PROJ)
            for a in range(16):
                kind, n = BESIDE[a]
                for sc in range(4):
                    if sc == 3:
                        splits_after(a - 1)
                    r = 4 * a + sc
                    act.wait_ge(pt_filled, r + 1)
                    if a >= 1:
                        act.wait_ge(o_filled, a)
                    nc.scalar.copy(pt_hi[:, sc, :], b_turn[r % 3][:, :]).then_inc(a_pthi, 1)
                if a + 1 < 16:
                    exps(a + 1)
                else:
                    for h in range(4):
                        act.wait_ge(o_copied, 8 + h + 1)
                        nc.scalar.copy(o_hi[1][:, h, :], q_of(h, 1)).then_inc(o1_hi, 1)
                if a == 1:
                    key_hi(N_PLAIN - 1)
                if kind == "p":
                    gain(n, b_side[0])
                    if n > N_PLAIN:
                        head_root(n - 1, b_side[1])
                elif kind == "s":
                    head_root(n, b_side[1])
                    for h in range(6, HEADS):
                        act.wait_ge(proj_done, NB * N_PROJ)
                        act.wait_ge(o_copied, h + 1)
                        nc.scalar.copy(o_hi[0][:, h, :], q_of(h, 0)).then_inc(o0_hi, 1)
                else:
                    if n >= 1:
                        square(3, n - 1, x_attn)
                act.wait_ge(o_filled, a + 1)
                nc.scalar.copy(q_of(a % 8, a // 8), b_out[:, :]).then_inc(o_copied, 1)
                if a == 9:
                    act.wait_ge(o0_pool, 6)
                    act.wait_ge(o0_split, 2)
                    split_hi(U_WO + 2)
            splits_after(15)
            split_next(unit_of("w", 6))
            for h in range(4, HEADS):
                act.wait_ge(o_copied, 8 + h + 1)
                nc.scalar.copy(o_hi[1][:, h, :], q_of(h, 1)).then_inc(o1_hi, 1)
            square(3, 6, x_attn)

            split_next(unit_of("w", 7))
            square(3, 7, x_attn)
            split_next(unit_of("w", 8))
            root(3, 0, bank[1])
            for c in range(KC):
                norm_hi(3, 0, c)
                square(3, 8 + c, x_attn)
                if c < KC - 1:
                    split_next(unit_of("w", 9 + c))
            act.wait_ge(o1_split, HEADS)
            for i in range(RING_WO, RING):
                split_hi(U_FFN1 + i)
            root(3, 1, b_down[0])
            swiglu(1)

            for i in range(NB * T // P):
                act.wait_ge(y_turned, 2 * i + 1)
                nc.scalar.copy(yout[:, i, 0:512], bank[(2 * i) % 4][:, :]).then_inc(y_act, 1)

        @block.vector
        def _(dve):
            def split_lo(u, step=None):
                dve.wait_ge(w_hi, u + 1 if step is None else step * (6 * BODIES) + u + 1)
                nc.vector.tensor_tensor(w_lo_t[:, slot(u), :], raw[:, u % RAW, :],
                                        w_hi_t[:, slot(u), :].bitcast(F32), ALU.subtract).then_inc(w_lo, 1)

            def inverse(k, b):
                dve.wait_ge(n_sqrt, 2 * (k - 1) + b + 1)
                nc.vector.reciprocal(stat[b][:, :], stat[b][:, :]).then_inc(n_rstd, 1)

            def norm_full(k, b, c):
                i = 16 * (k - 1) + KC * b + c
                dve.wait_ge(n_rstd, 2 * (k - 1) + b + 1)
                if i >= 2:
                    dve.wait_ge(n_lo, i - 1)
                g = GAIN[k] + c
                nc.vector.scalar_tensor_tensor(full[i % 2][:, :], x[:, c, tok(b)], vec[:, g:g + 1], stat[b][:, :],
                                               ALU.mult, ALU.mult).then_inc(n_full, 1)

            def norm_lo(k, b, c):
                i = 16 * (k - 1) + KC * b + c
                dve.wait_ge(n_hi, i + 1)
                nc.vector.tensor_tensor(h_lo[k][b][:, c, :], full[i % 2][:, :], h_hi[k][b][:, c, :].bitcast(F32),
                                        ALU.subtract).then_inc(n_lo, 1)

            def norm_batch(k, b, beside):
                for c in range(4):
                    beside(c)
                inverse(k, b)
                for c in range(KC):
                    if c + 4 < KC:
                        beside(c + 4)
                    norm_full(k, b, c)
                    if c >= 1:
                        norm_lo(k, b, c - 1)
                norm_lo(k, b, KC - 1)


            def token_inverse(b):
                dve.wait_ge(t_root, b + 1)
                cols = tok_rms[:, NT * b:NT * (b + 1)]
                nc.vector.reciprocal(cols, cols).then_inc(t_inv, 1)

            def pooled_lo(b, c):
                q = KC * b + c
                dve.wait_ge(m_hi, q + 1)
                nc.vector.tensor_tensor(h_lo[0][b][:, c, :], bank[q % 3][:, :], h_hi[0][b][:, c, :].bitcast(F32),
                                        ALU.subtract).then_inc(m_lo, 1)

            def add_mixed(b, c):
                q = KC * b + c
                dve.wait_ge(m_filled, q + 1)
                xc = x[:, c, tok(b)]
                nc.vector.scalar_tensor_tensor(xc, b_down[q % 4][:, :], vec[:, V_PS + c:V_PS + c + 1], xc,
                                               ALU.mult, ALU.add).then_inc(m_x, 1)

            def token_norm(b, i):
                if i == 0:
                    dve.wait_ge(t_inv, b + 1)
                nc.vector.tensor_scalar(xrms[b][i // 2][:, i % 2, :], xin[b][:, i, :],
                                        tok_rms[:, NT * b + i:NT * b + i + 1], None, ALU.mult).then_inc(t_norm, 1)

            def gained_lo(u):
                dve.wait_ge(w_hi, u + 1)
                for j in range(4):
                    blk = slice(256 * j, 256 * (j + 1))
                    ins = nc.vector.scalar_tensor_tensor(
                        w_lo_t[:, slot(u), blk], raw[:, u, blk], vec[:, V_MIX + 4 * u + j:V_MIX + 4 * u + j + 1],
                        w_hi_t[:, slot(u), blk].bitcast(F32), ALU.mult, ALU.subtract)
                ins.then_inc(w_lo, 1)

            def move_x(c):
                dve.wait_ge(x_turned, c + 1)
                nc.vector.tensor_scalar(x[:, c, tok(0)], b_down[c % 4][:, :], vec[:, V_BS + c:V_BS + c + 1], None,
                                        ALU.add).then_inc(x_moved_dve, 1)

            token_inverse(0)
            token_norm(0, 0)
            token_norm(0, 1)
            dve.wait_ge(vec_turned, 1)
            nc.vector.tensor_copy(vec[:, 0:N_VEC], bank[0][:, 0:N_VEC]).then_inc(vec_ready, 1)
            dve.wait_ge(vec_ready, 1)
            nc.vector.tensor_tensor(vec[:, V_BS:V_BS + KC], vec[:, V_PB:V_PB + KC], vec[:, V_PS:V_PS + KC],
                                    ALU.mult).then_inc(vec_ready, 1)
            token_norm(0, 2)
            token_norm(0, 3)
            dve.wait_ge(vec_ready, 2)
            for c in range(4, KC):
                move_x(c)
            pooled_lo(0, 0)
            pooled_lo(0, 1)
            gained_lo(0)
            pooled_lo(0, 2)
            pooled_lo(0, 3)
            gained_lo(1)
            add_mixed(0, 0)
            add_mixed(0, 1)
            pooled_lo(0, 4)
            pooled_lo(0, 5)
            token_inverse(1)
            token_norm(1, 0)
            add_mixed(0, 2)
            add_mixed(0, 3)
            token_norm(1, 1)
            pooled_lo(0, 6)
            pooled_lo(0, 7)
            token_norm(1, 2)
            split_lo(U_FFN0)
            add_mixed(0, 4)
            token_norm(1, 3)
            for c in range(5, KC):
                add_mixed(0, c)
            for c in range(3):
                pooled_lo(1, c)
            inverse(1, 0)
            split_lo(U_FFN0 + 1)
            pooled_lo(1, 3)
            for c in (0, 2):
                norm_full(1, 0, c)
                norm_full(1, 0, c + 1)
                norm_lo(1, 0, c)
                norm_lo(1, 0, c + 1)
                pooled_lo(1, 4 + c)
                pooled_lo(1, 5 + c)
                add_mixed(1, c)
                add_mixed(1, c + 1)
            for c in (4, 6):
                norm_full(1, 0, c)
                norm_full(1, 0, c + 1)
                norm_lo(1, 0, c)
                norm_lo(1, 0, c + 1)
                add_mixed(1, c)
                add_mixed(1, c + 1)
            for i in range(2, 5):
                split_lo(U_FFN0 + i)

            def hidden(layer, g, t, j=None):
                c, b = t % 2, t // 2
                i = 4 * g + t
                n = N_TILE * layer + i
                step = 0 if j is None else j * (4 * BODIES)
                dve.wait_ge(silu_done, step + n + 1)
                dve.wait_ge(up_done, step + n + 1)
                if i >= 2:
                    dve.wait_ge(act_lo_done, step + n - 1)
                else:
                    dve.wait_ge(n_lo, 32 * layer + KC + (FIRST_TILE[layer] if t == 0 else KC))
                nc.vector.tensor_tensor(full[t % 2][:, :], silu_t[t % 2][:, :], b_up[t % 2][:, :],
                                        ALU.mult).then_inc(prod_done, 1)
                dve.wait_ge(act_hi_done, step + n + 1)
                nc.vector.tensor_tensor(act_lo[:, g % 2, c, tok(b)], full[t % 2][:, :],
                                        act_hi[:, g % 2, c, tok(b)].bitcast(F32), ALU.subtract
                                        ).then_inc(act_lo_done, 1)

            def add_down(layer, g, i, j=None):
                q = N_DOWN * layer + 16 * g + i
                step = 0 if j is None else j * (16 * BODIES)
                dve.wait_ge(down_filled, step + q + 1)
                xc = x[:, i % KC, tok(i // KC)]
                nc.vector.tensor_tensor(xc, b_down[i % 4][:, :], xc, ALU.add).then_inc(down_added, 1)

            def group(layer, g, j=None):
                for t in range(4):
                    if g == 0 and t == 0:
                        k = 2 * layer + 1
                        inverse(k, 1)
                        if layer == 0:
                            split_lo(U_FFN0 + 5)
                        for c in range(KC):
                            if c == FIRST_TILE[layer]:
                                if c > 0:
                                    norm_lo(k, 1, c - 1)
                                hidden(layer, 0, 0)
                                dve.wait_ge(act_lo_done, N_TILE * layer + 1)
                            norm_full(k, 1, c)
                            if c >= 1 and c != FIRST_TILE[layer]:
                                norm_lo(k, 1, c - 1)
                        norm_lo(k, 1, KC - 1)
                    else:
                        hidden(layer, g, t, j)
                    if t >= 2:
                        for up in range(2):
                            u = gu_unit(layer, g, t - 2, up) + RING
                            if u < U_FFN[layer] + N_FFN or (layer == 0 and slot(u) < 2):
                                split_lo(u, j)
                if g >= 1:
                    for i in range(16):
                        add_down(layer, g - 1, i, j)
                    if down_unit(layer, g - 1, 0) + RING < U_FFN[layer] + N_FFN:
                        for c in range(GF):
                            split_lo(down_unit(layer, g - 1, c) + RING, j)

            def swiglu(layer):
                group(layer, 0)
                with dve.Fori(0, LOOPS) as j:
                    for g in range(1, 1 + BODIES):
                        group(layer, g, j)
                for g in range(FIRST_PEELED, NG):
                    group(layer, g)

            swiglu(0)
            for i in range(KC):
                add_down(0, NG - 1, i)
            norm_batch(2, 0, lambda c: add_down(0, NG - 1, KC + c))

            def head_inverse(p):
                inv = qsq[p % 2][:, :] if p % N_PROJ < KVH else q_inv[:, q_cols(p)]
                dve.wait_ge(p_sqrt, p + 1)
                nc.vector.reciprocal(inv, inv).then_inc(p_r, 1)

            def rope(p):
                s, b, j = p % 2, p // N_PROJ, p % N_PROJ
                dve.wait_ge(rot_in[s], 64 * (p // 2 + 1))
                dve.wait_ge(tables_in, 32)
                nc.vector.tensor_tensor(rot[s][:, :], rot[s][:, :], sin_t[:, :], ALU.mult).then_inc(p_sin, 1)
                dve.wait_ge(p_cos, p + 1)
                dve.wait_ge(p_sin, p + 1)
                if j < KVH:
                    nc.vector.tensor_tensor(qg[s][:, :], qg[s][:, :], rot[s][:, :], ALU.add).then_inc(p_sum, 1)
                    dve.wait_ge(p_sum, KVH * b + j + 1)
                    dve.wait_ge(p_r, p + 1)
                    nc.vector.tensor_tensor(rot[s][:, :], qg[s][:, :], qsq[s][:, :], ALU.mult).then_inc(p_fin, 1)
                else:
                    nc.vector.tensor_tensor(q_of(j - KVH, b), qg[s][:, :], rot[s][:, :], ALU.add).then_inc(p_done, 1)

            def key_lo(p):
                s, b, j = p % 2, p // N_PROJ, p % N_PROJ
                dve.wait_ge(p_hi, KVH * b + j + 1)
                nc.vector.tensor_tensor(k_lo[:, j, tok(b)], rot[s][:, :], k_hi[:, j, tok(b)].bitcast(F32),
                                        ALU.subtract).then_inc(p_done, 1)

            def split_next(i):
                split_lo(following(i))

            def values_lo(b, banks):
                for t in range(2):
                    dve.wait_ge(v_hi_done, 2 * b + t + 1)
                    tt = slice(4 * b + 2 * t, 4 * b + 2 * t + 2)
                    nc.vector.tensor_tensor(v_lo[:, tt, :], banks[t][:, :].rearrange("p (t f) -> p t f", t=2),
                                            v_hi[:, tt, :].bitcast(F32), ALU.subtract).then_inc(v_lo_done, 1)

            split_next(0)
            inverse(2, 1)
            for c in range(KC):
                norm_full(2, 1, c)
                if c == 3:
                    split_next(1)
                elif c == 5:
                    head_inverse(0)
            split_next(2)
            head_inverse(1)
            split_next(3)
            rope(0)
            key_lo(0)
            rope(1)
            key_lo(1)
            values_lo(0, b_down)
            split_next(4)
            for p in range(3, N_PLAIN):
                head_inverse(p - 1)
                if p < N_PLAIN - 1:
                    rope(p - 1)
                split_next(unit_of("p", p))

            def row_max(s):
                dve.wait_ge(s_filled, s + 1)
                if s >= 8:
                    dve.wait_ge(a_prob, s - 7)
                col = slice(s % 8, s % 8 + 1)
                nc.vector.tensor_reduce(raw_max[:, col], b_score[s % 2][:, :], AX.X, ALU.max,
                                        negate=True).then_inc(a_rawmax, 1)
                dve.wait_ge(a_rawmax, s + 1)
                if s % (T // P) == 0:
                    a = s // (T // P)
                    dve.wait_ge(p_r, N_PROJ * (a // HEADS) + KVH + a % HEADS + 1)
                nc.vector.tensor_tensor(nmax[:, col], raw_max[:, col], q_inv[:, s:s + 1], ALU.mult).then_inc(a_max, 1)

            def normalise(s):
                dve.wait_ge(a_exp, s + 1)
                col = slice(s % 8, s % 8 + 1)
                nc.vector.reciprocal(rinv[:, col], rsum[:, col]).then_inc(a_rinv, 1)
                dve.wait_ge(a_rinv, s + 1)
                nc.vector.tensor_scalar(prob[:, s % 4, :], prob[:, s % 4, :], rinv[:, col], None,
                                        ALU.mult).then_inc(a_prob, 1)

            def softmax(a, part):
                for i in range(2 * part, 2 * part + 2):
                    row_max(4 * a + i)
                    if i > 0:
                        normalise(4 * a + i - 1)
                if part == 1:
                    normalise(4 * a + 3)

            def add_wo(w):
                dve.wait_ge(wo_filled, w + 1)
                xc = x[:, w % KC, tok(w // KC)]
                nc.vector.tensor_tensor(xc, b_side[w % 2][:, :], xc, ALU.add).then_inc(wo_added, 1)

            def splits_after(a):
                if 0 <= a < 8:
                    split_next(unit_of(*BESIDE[a]))
                elif a == 9:
                    split_lo(U_WO + 3)
                elif a >= 10:
                    split_next(unit_of("w", a - 10))

            softmax(0, 0)
            rope(N_PROJ)
            softmax(0, 1)
            split_next(N_QKV + 2)
            values_lo(1, b_side)
            split_next(N_QKV + 3)
            key_lo(N_PROJ)
            for a in range(16):
                kind, n = BESIDE[a]
                for sc in range(4):
                    if sc == 3:
                        splits_after(a - 1)
                    r = 4 * a + sc
                    dve.wait_ge(a_pthi, r + 1)
                    nc.vector.tensor_tensor(pt_lo[:, sc, :], b_turn[r % 3][:, :], pt_hi[:, sc, :].bitcast(F32),
                                            ALU.subtract).then_inc(a_ptlo, 1)
                if a + 1 < 16:
                    softmax(a + 1, 0)
                if a == 1:
                    rope(N_PLAIN - 1)
                if a + 1 < 16:
                    softmax(a + 1, 1)
                else:
                    for h in range(4):
                        dve.wait_ge(o1_hi, h + 1)
                        nc.vector.tensor_tensor(o_lo[1][:, h, :], q_of(h, 1), o_hi[1][:, h, :].bitcast(F32),
                                                ALU.subtract).then_inc(o1_split, 1)
                if a == 1:
                    key_lo(N_PLAIN - 1)
                if kind == "p" and n == N_PLAIN:
                    head_inverse(n - 1)
                elif kind == "p":
                    rope(n - 1)
                    head_inverse(n - 1)
                elif kind == "s":
                    rope(n)
                    head_inverse(n)
                    for h in range(6, HEADS):
                        dve.wait_ge(o0_hi, h - 5)
                        nc.vector.tensor_tensor(o_lo[0][:, h, :], q_of(h, 0), o_hi[0][:, h, :].bitcast(F32),
                                                ALU.subtract).then_inc(o0_split, 1)
                else:
                    add_wo(n)
                if a == 9:
                    split_lo(U_WO + 2)
            splits_after(15)
            split_next(unit_of("w", 6))
            for h in range(4, HEADS):
                dve.wait_ge(o1_hi, h + 1)
                nc.vector.tensor_tensor(o_lo[1][:, h, :], q_of(h, 1), o_hi[1][:, h, :].bitcast(F32),
                                        ALU.subtract).then_inc(o1_split, 1)

            add_wo(7)
            split_next(unit_of("w", 7))
            add_wo(8)
            split_next(unit_of("w", 8))
            inverse(3, 0)
            norm_full(3, 0, 0)
            for c in range(1, KC):
                norm_full(3, 0, c)
                norm_lo(3, 0, c - 1)
                add_wo(8 + c)
                split_next(unit_of("w", 8 + c))
            norm_lo(3, 0, KC - 1)
            for i in range(RING_WO, RING):
                split_lo(U_FFN1 + i)
            swiglu(1)
            def copy_y(i):
                dve.wait_ge(y_turned, 2 * i + 2)
                nc.vector.tensor_copy(yout[:, i, 512:1024], bank[(2 * i + 1) % 4][:, :]).then_inc(y_dve, 1)

            for i in range(KC + 3):
                add_down(1, NG - 1, i)
            for i in range(NT):
                copy_y(i)
            for i in range(KC + 3, 2 * KC):
                add_down(1, NG - 1, i)
            for i in range(NT, NB * NT):
                copy_y(i)

        @block.gpsimd
        def _(pool):
            nc.gpsimd.memset(ident[:, :], 0.0).then_inc(ident_made, 1)
            pool.wait_ge(ident_made, 1)
            nc.gpsimd.affine_select(out=ident[:, :], in_=ident[:, :], compare_op=ALU.not_equal, fill=1.0,
                                    base=0, pattern=[[-1, P]], channel_multiplier=1).then_inc(ident_made, 1)
            nc.gpsimd.memset(ones[:, :], 1.0).then_inc(ones_made, 1)
            nc.gpsimd.memset(epst[:, 0:1], EPS).then_inc(eps_made, 1)
            nc.gpsimd.memset(epst[:, 1:2], EPS * HD).then_inc(eps_made, 1)

            def add_squares(k, r):
                c, b = SEQ[r]
                if c == 0:
                    return
                i = acc_index(k, r)
                pool.wait_ge(n_sq, 16 * (k - 1) + r + 1)
                if i >= 2:
                    pool.wait_ge(n_acc, i - 1)
                nc.gpsimd.tensor_tensor(out=stat[b][:, :], in0=stat[b][:, :], in1=sqr[i % 2][:, :],
                                        op=ALU.add).then_inc(n_acc, 1)

            for r in range(16):
                add_squares(1, r)
            for r in range(16):
                add_squares(2, r)

            pool.wait_ge(n_lo, KC + 2 * KC)
            for c in range(KC):
                i = 16 + KC + c
                pool.wait_ge(n_hi, i + 1)
                nc.gpsimd.tensor_tensor(out=h_lo[2][1][:, c, :], in0=full[i % 2][:, :],
                                        in1=h_hi[2][1][:, c, :].bitcast(F32), op=ALU.subtract).then_inc(n_lo, 1)

            def times_cos(p):
                pool.wait_ge(rot_in[p % 2], 64 * (p // 2 + 1))
                nc.gpsimd.tensor_tensor(out=qg[p % 2][:, :], in0=qg[p % 2][:, :], in1=cos_t[:, :],
                                        op=ALU.mult).then_inc(p_cos, 1)

            pool.wait_ge(tables_in, 32)
            for p in range(N_PROJ):
                times_cos(p)

            def split_q(a):
                pool.wait_ge(p_done, N_PROJ * (a // 8) + KVH + a % 8 + 1)
                if a == 0:
                    pool.wait_ge(proj_done, N_PROJ)
                    pool.wait_ge(v_filled, 2)
                if a >= 2:
                    pool.wait_ge(s_filled, 4 * (a - 1))
                src = q_of(a % 8, a // 8)
                nc.gpsimd.tensor_scalar(qs_hi[:, a % 2, :], src, 1.0, 0.0, ALU.mult, ALU.add).then_inc(a_qhi, 1)
                pool.wait_ge(a_qhi, a + 1)
                nc.gpsimd.tensor_tensor(out=qs_lo[:, a % 2, :], in0=src, in1=qs_hi[:, a % 2, :].bitcast(F32),
                                        op=ALU.subtract).then_inc(a_q, 1)

            split_q(0)
            split_q(1)
            times_cos(N_PROJ)
            times_cos(N_PROJ + 1)
            for a in range(16):
                if a + 2 < 16:
                    split_q(a + 2)
                kind, n = BESIDE[a]
                if kind == "p":
                    times_cos(n)
                elif kind == "w" and n >= 1:
                    add_squares(3, n - 1)
                if a == 8:
                    pool.wait_ge(proj_done, NB * N_PROJ)
                    pool.wait_ge(o_copied, 8)
                    for h in range(6):
                        nc.gpsimd.tensor_scalar(o_hi[0][:, h, :], q_of(h, 0), 1.0, 0.0, ALU.mult,
                                                ALU.add).then_inc(o0_pool_hi, 1)
                        pool.wait_ge(o0_pool_hi, h + 1)
                        nc.gpsimd.tensor_tensor(out=o_lo[0][:, h, :], in0=q_of(h, 0),
                                                in1=o_hi[0][:, h, :].bitcast(F32), op=ALU.subtract
                                                ).then_inc(o0_pool, 1)
            for r in range(6, 16):
                add_squares(3, r)


def tables():
    import numpy as np
    grid_w, axis = 64, HD // 2
    t = np.arange(T)
    inv = (np.float32(10000.0) ** (-np.arange(0, axis, 2, dtype=np.float32) / np.float32(axis))).astype(np.float32)
    cos, sin = np.zeros((HD, T), np.float32), np.zeros((HD, T), np.float32)
    for d in range(HD):
        pos = (t // grid_w if d < axis else t % grid_w).astype(np.float32)
        ang = (pos * inv[d % 32]).astype(np.float32).astype(np.float64)
        cos[d] = np.cos(ang)
        sin[d] = np.sin(ang) * (-1.0 if d % axis < 32 else 1.0)
    band = np.zeros((P, len(WINDOWS), 3, BAND), np.float32)
    for g, w in enumerate(WINDOWS):
        for kind, i in enumerate((0, 1, NT - 1)):
            first = max(i * P - REACH, 0)
            for tt in range(first, min((i + 1) * P + REACH, T)):
                lo, hi = max(tt - w // 2, 0), min(tt + w // 2, T)
                for s in range(max(lo, i * P), min(hi, (i + 1) * P)):
                    band[s - i * P, g, kind, tt - first] = np.float32(1.0) / np.float32(hi - lo)
                if i * P <= tt < (i + 1) * P:
                    band[tt - i * P, g, kind, tt - first] -= np.float32(1.0)
    return cos, sin, band


_INS = ["x_prompt", "x_sample", "norm_mix", "norm_ffn", "pool_w", "pool_b", "pool_scale", "attn_w_qkv",
        "attn_q_gain", "attn_k_gain", "attn_w_o", "ffn_w_gate_up", "ffn_w_down"]


def kernel(**inputs):
    import numpy as np
    import concourse.bacc as bacc
    from concourse.bass_utils import run_bass_kernel_spmd as run

    nc = bacc.Bacc("TRN2", target_bir_lowering=False, num_devices=1)
    arrays, args = {}, []
    cos, sin, band = tables()
    for name, a in [(n, np.ascontiguousarray(inputs[n])) for n in _INS] + [
            ("rope_cos", cos), ("rope_sin", sin), ("band_tab", band)]:
        arrays[f"in_{name}"] = a
        args.append(nc.dram_tensor(f"in_{name}", a.shape, mybir.dt.from_np(a.dtype), kind="ExternalInput").ap())
    for name in ("y_prompt", "y_sample"):
        args.append(nc.dram_tensor(f"out_{name}", (1, T, D), F32, kind="ExternalOutput").ap())
    build(nc, *args)
    r = run(nc, [arrays], core_ids=[0])
    return r.results[0]["out_y_prompt"], r.results[0]["out_y_sample"]
```
